# Optimizing a Trainium2 kernel written in Bass

```python
import jax
import jax.numpy as jnp
from jax import lax
import numpy as np

D_MODEL = 1024
BATCH = 1
SEQ = 1024
DEPTH = 1

N_META = 16
HG_HEADS = 8
HG_DK = 128
HG_DV = D_MODEL // HG_HEADS
HG_KWIDTH = HG_HEADS * HG_DK
HG_VWIDTH = HG_HEADS * HG_DV
CHUNK = 64
SUB = 16
POOL_WINDOWS = (2, 4, 8, 16)
POOL_GROUPS = len(POOL_WINDOWS)
POOL_WIDTH = D_MODEL
POOL_GDIM = POOL_WIDTH // POOL_GROUPS
EPS = 1e-6
IN_SIZES = (HG_KWIDTH, HG_KWIDTH, HG_VWIDTH, HG_VWIDTH, POOL_WIDTH, POOL_WIDTH, D_MODEL, D_MODEL)
IN_COLS = sum(IN_SIZES)

kernel_name = 'hybrid_hgrn2_pool_block'

def rms_norm(x, w):
    xf = x.astype(jnp.float32)
    y = xf * lax.rsqrt(jnp.mean(xf * xf, axis=-1, keepdims=True) + EPS)
    return (y * w.astype(jnp.float32)).astype(x.dtype)

def to_chunks(t, dh):
    B = t.shape[0]
    t = jnp.pad(t, ((0, 0), (CHUNK - N_META, 0), (0, 0)))
    n = t.shape[1] // CHUNK
    return t.reshape(B, n, CHUNK, HG_HEADS, dh).transpose(1, 0, 3, 2, 4)

def hgrn2_chunkwise(q, k, v, log_f):
    _, B, H, C, DK = q.shape
    DV = v.shape[-1]
    ns = C // SUB
    causal = jnp.tril(jnp.ones((SUB, SUB), dtype=bool))
    earlier = jnp.tril(jnp.ones((ns, ns), dtype=bool), -1)
    diag = jnp.eye(ns, dtype=jnp.float32)

    def step(S, inp):
        qc, kc, vc, gc = inp
        b = jnp.cumsum(gc, axis=2)
        o_inter = jnp.einsum('bhtk,bhkv->bhtv', qc * jnp.exp(b), S)
        qs = qc.reshape(B, H, ns, SUB, DK)
        ks = kc.reshape(B, H, ns, SUB, DK)
        bs = b.reshape(B, H, ns, SUB, DK)
        ref = bs[:, :, :, 0]
        q_ref = qs * jnp.exp(bs - ref[:, :, :, None])
        expo = jnp.where(earlier[None, None, :, :, None, None],
                         ref[:, :, :, None, None, :] - bs[:, :, None, :, :, :], -jnp.inf)
        k_ref = ks[:, :, None] * jnp.exp(expo)
        a_off = jnp.einsum('bhitk,bhijsk->bhitjs', q_ref, k_ref)
        dexp = jnp.where(causal[:, :, None],
                         bs[:, :, :, :, None, :] - bs[:, :, :, None, :, :], -jnp.inf)
        a_diag = jnp.einsum('bhitk,bhitsk,bhisk->bhits', qs, jnp.exp(dexp), ks)
        a = (a_off + a_diag[:, :, :, :, None, :] * diag[:, None, :, None]).reshape(B, H, C, C)
        o = o_inter + jnp.einsum('bhts,bhsv->bhtv', a, vc)
        b_last = b[:, :, -1]
        S_new = jnp.exp(b_last)[..., None] * S + jnp.einsum(
            'bhsk,bhsv->bhkv', kc * jnp.exp(b_last[:, :, None] - b), vc)
        return S_new, o

    S0 = jnp.zeros((B, H, DK, DV), jnp.float32)
    _, o = lax.scan(step, S0, (q, k, v, log_f))
    return o

def causal_multiscale_pool(u):
    B, L, _ = u.shape
    ug = u.astype(jnp.float32).reshape(B, L, POOL_GROUPS, POOL_GDIM)
    cs = jnp.cumsum(ug, axis=1)
    pos = jnp.arange(L)
    outs = []
    for g, w in enumerate(POOL_WINDOWS):
        c = cs[:, :, g]
        lagged = jnp.pad(c, ((0, 0), (w, 0), (0, 0)))[:, :L]
        cnt = jnp.minimum(pos + 1, w).astype(jnp.float32)[None, :, None]
        outs.append((c - lagged) / cnt - ug[:, :, g])
    return jnp.stack(outs, axis=2)

def setup_inputs(seed: int = 0) -> dict:
    key = jax.random.key(seed)
    ks = jax.random.split(key, 13)
    nrm = jax.random.normal
    d = D_MODEL
    f32 = jnp.float32
    return {
        'x': nrm(ks[0], (BATCH, SEQ, d), f32),
        'meta_tokens': nrm(ks[1], (N_META, d), f32),
        'norm_w': 1.0 + 0.02 * nrm(ks[2], (DEPTH, d), f32),
        'w_in': nrm(ks[3], (DEPTH, d, IN_COLS), f32) * d ** -0.5,
        'b_in': 0.01 * nrm(ks[4], (DEPTH, IN_COLS), f32),
        'lb_logits': 0.1 * nrm(ks[5], (DEPTH + 1, HG_KWIDTH), f32),
        'hg_norm_w': 1.0 + 0.02 * nrm(ks[6], (DEPTH, HG_VWIDTH), f32),
        'pool_w': nrm(ks[7], (DEPTH, POOL_GROUPS, POOL_GDIM, POOL_GDIM), f32) * POOL_GDIM ** -0.5,
        'pool_scale': 1.0 + 0.02 * nrm(ks[8], (DEPTH, POOL_WIDTH), f32),
        'w_down_hg': nrm(ks[9], (DEPTH, HG_VWIDTH, d), f32) * HG_VWIDTH ** -0.5,
        'w_down_pool': nrm(ks[10], (DEPTH, POOL_WIDTH, d), f32) * POOL_WIDTH ** -0.5,
        'w_out': nrm(ks[11], (DEPTH, d, d), f32) * d ** -0.5,
        'final_norm_w': 1.0 + 0.02 * nrm(ks[12], (d,), f32),
    }

def reference(x, meta_tokens, norm_w, w_in, b_in, lb_logits, hg_norm_w, pool_w, pool_scale,
              w_down_hg, w_down_pool, w_out, final_norm_w):
    f32 = jnp.float32
    B = x.shape[0]
    meta = jnp.broadcast_to(meta_tokens.astype(x.dtype)[None], (B, N_META, D_MODEL))
    z = jnp.concatenate([meta, x], axis=1)
    L = z.shape[1]
    lower_bounds = jnp.cumsum(jax.nn.softmax(lb_logits.astype(f32), axis=0), axis=0)
    split_at = np.cumsum(IN_SIZES)[:-1].tolist()
    for l in range(DEPTH):
        h = rms_norm(z, norm_w[l])
        p = (h @ w_in[l] + b_in[l]).astype(f32)
        q, fz, iv, g_hg, u, g_pool, m_hg, m_pool = jnp.split(p, split_at, axis=-1)
        lb = lower_bounds[l]
        log_f = jnp.log(lb + (1.0 - lb) * jax.nn.sigmoid(fz))
        k = (1.0 - lb) * jax.nn.sigmoid(-fz)
        o = hgrn2_chunkwise(to_chunks(q, HG_DK), to_chunks(k, HG_DK),
                            to_chunks(iv, HG_DV), to_chunks(log_f, HG_DK))
        o = o.transpose(1, 0, 3, 2, 4).reshape(B, -1, HG_HEADS, HG_DV)[:, CHUNK - N_META:]
        o = rms_norm(o, hg_norm_w[l].reshape(HG_HEADS, HG_DV)).reshape(B, L, HG_VWIDTH)
        y_hg = (o * jax.nn.silu(g_hg)) @ w_down_hg[l].astype(f32)
        pooled = causal_multiscale_pool(u)
        mixed = jnp.einsum('blgc,gcd->blgd', pooled, pool_w[l].astype(f32)).reshape(B, L, POOL_WIDTH)
        y_pool = (mixed * pool_scale[l].astype(f32) * jax.nn.silu(g_pool)) @ w_down_pool[l].astype(f32)
        merged = jax.nn.sigmoid(m_hg) * y_hg + jax.nn.sigmoid(m_pool) * y_pool
        z = z + (merged @ w_out[l].astype(f32)).astype(z.dtype)
    return rms_norm(z, final_norm_w)[:, N_META:]


_drawn_inputs = setup_inputs


def setup_inputs(seed=0):
    import zlib

    import numpy as np

    out = dict(_drawn_inputs(seed))
    spreads = {}
    factors = {'meta_tokens': 4.583,
     'norm_w': 3.662,
     'b_in': 6.119,
     'hg_norm_w': 8.0,
     'pool_scale': 8.0,
     'final_norm_w': 2.89}
    for name, (base, spread) in spreads.items():
        noise = np.random.default_rng([zlib.crc32(name.encode()), seed]).standard_normal(out[name].shape)
        drawn = base * np.exp(spread * noise) if base else spread * noise
        out[name] = jnp.asarray(drawn.astype(out[name].dtype))
    for name, factor in factors.items():
        out[name] = (out[name] * factor).astype(out[name].dtype)
    return out
```

```python
from contextlib import ExitStack

import concourse.bass as bass
from concourse import mybir

ALU = mybir.AluOpType
ACT = mybir.ActivationFunctionType
AX = mybir.AxisListType
F32 = mybir.dt.float32
F32R = mybir.dt.float32r
U8 = mybir.dt.uint8
ds = bass.ds

P = 128
D = 1024
NK = D // P
SEQ = 1024
META = 16
L = META + SEQ
HEADS = 8
CHUNKS = SEQ // P
LEVELS = 7
HALF = 512
WINDOWS = (2, 4, 8, 16)
EPS = 1e-6

Q, F, V, G, U, PG, MH, MP = range(8)

WITH_META = ((0, 348), (348, 346), (694, 346))
NO_META = ((META, HALF), (META + HALF, HALF))

BLK_TAIL, BLK_MIX, BLK_POOL, BLK_DOWN, BLK_OUT, BLKS = 36, 40, 56, 72, 80, 88
U_TAIL, U_MIX, U_POOL, U_DOWN, U_OUT, UNITS = 88, 96, 128, 184, 200, 216
MASKS = 7
LEVEL_AT = (2, 4, 7, 9, 10, 12, 13)
BANKS8 = (0, 1, 2, 3, 0, 1, 2, 3)
BANKS10 = (0, 1, 2, 0, 1, 2, 0, 1, 2, 3)
BANKS14 = (0, 1, 2, 3, 0, 1, 2, 3, 0, 1, 2, 0, 1, 3)


def stream_order():
    order = []
    for j in range(HEADS):
        order += [("in", 8 * F + j), ("in", 8 * V + j), ("in", 8 * Q + j)]
        if j:
            order.append(("in", 8 * G + j - 1))
    order += [("in", 8 * MP + n) for n in range(4)] + [("in", 8 * G + HEADS - 1)]
    order += [("in", 8 * MP + n) for n in range(4, 8)]
    for n in range(8):
        order += [("in", 8 * MH + n), ("down_hg", n)]
    for g in range(4):
        order += [("in", 8 * U + 2 * g), ("in", 8 * U + 2 * g + 1), ("in", 8 * PG + 2 * g),
                  ("in", 8 * PG + 2 * g + 1)]
    order += [("down_pool", n) for n in range(8)]
    order += [("out", n) for n in range(8)]
    return order


def after(eng, sem, count):
    if not isinstance(count, int) or count > 0:
        eng.wait_ge(sem, count)


def first_unit(j):
    return 0 if isinstance(j, int) and j == 0 else j * 10 - 2


def first_block(j):
    return 0 if isinstance(j, int) and j == 0 else j * 4 - 1


class Steps:

    def __init__(self, eng, sem):
        self.eng, self.sem, self.base, self.n = eng, sem, 0, 0

    def mark(self, instruction):
        instruction.then_inc(self.sem, 1)
        self.n += 1

    def settle(self):
        self.eng.wait_ge(self.sem, self.base + self.n)

    def enter(self, i, i0, per):
        self.start = self.base + self.n
        self.base, self.n = (i - i0) * per + self.start, 0

    def leave(self, per, times):
        assert self.n == per, (self.n, per)
        self.base, self.n = self.start + per * times, 0


def hybrid_block(nc, x, meta, norm_w, wstream, pool_w, b_in, lb_logits, hg_norm_w, pool_scale, final_norm_w, out):
    names = ExitStack()
    with names:
        sem_names = [
            "params_loaded", "norm_row_loaded", "x_loaded0", "x_loaded1", "x_loaded2", "raw_loaded0", "raw_loaded1",
            "lb_shifted", "lb_exp", "consts_made", "masks_made", "masks_spread", "pool_step",
            "x_squared", "x_mean", "x_rstd", "h_row", "h_tr", "h_hi_done", "h_lo_done",
            "w_hi_ready", "w_lo_ready", "acc_done", "acc_read",
            "prepared", "v_tr", "v_copied", "level_mm", "level_done", "k_tr", "k_copied", "kv_mm",
            "state_done", "o_mm", "o_squared", "o_mean", "o_rstd", "o_normed", "o_tr", "a_done", "gate_done",
            "smp_stored0", "smp_stored1", "part_made", "part_stored0", "part_stored1",
            "pooled_done", "pgate_done", "pw_loaded", "pw_hi_done", "pw_lo_done", "c_done",
            "spill_loaded0", "spill_loaded1", "merged_done", 
            "fnw_loaded", "xr_loaded0", "xr_loaded1", "z_done", "z_squared", "z_mean", "z_rstd",
            "row_done", "row_stored0", "row_stored1", "vec_step", "act_step",
        ]
        S = {n: names.enter_context(nc.semaphore(n)) for n in sem_names}

        here = [16512]

        def at(name, shape, dtype, offset=None):
            size = 4 if dtype != U8 else 1
            for n in shape[1:]:
                size *= n
            if offset is None:
                offset = here[0]
                here[0] += (size + 31) // 32 * 32
            return nc.alloc_sbuf_tensor_at(name, shape, dtype, offset=offset), offset

        h_hi, _ = at("h_hi", [P, NK, L], F32R)
        h_lo, _ = at("h_lo", [P, NK, L], F32R)
        a_hi, a_hi_at = at("a_hi", [P, NK, SEQ], F32R)
        a_lo, a_lo_at = at("a_lo", [P, NK, SEQ], F32R)
        raw, _ = at("raw", [P, 2, D], F32)
        w_hi, _ = at("w_hi", [P, 2, D], F32R)
        w_lo, _ = at("w_lo", [P, 2, D], F32R)
        bias, _ = at("bias", [P, 8, 8], F32)
        cur, _ = at("cur", [P, 3, 8], F32)
        lb, _ = at("lb", [P, HEADS], F32)
        one_minus_lb, _ = at("one_minus_lb", [P, HEADS], F32)
        hgw, _ = at("hgw", [P, HEADS], F32)
        psc, _ = at("psc", [P, NK], F32)
        logits, _ = at("logits", [P, 2, HEADS], F32)
        lexp, _ = at("lexp", [P, 2, HEADS], F32)
        lmax, _ = at("lmax", [P, HEADS], F32)
        x_ss, _ = at("x_ss", [P, 16], F32)
        x_ms, _ = at("x_ms", [P, 16], F32)
        x_rs, _ = at("x_rs", [P, 16], F32)
        o_ss, _ = at("o_ss", [P, CHUNKS], F32)
        o_ms, _ = at("o_ms", [P, CHUNKS], F32)
        o_rs, _ = at("o_rs", [P, CHUNKS], F32)
        minus_half, _ = at("minus_half", [P, 16], F32)
        ident, _ = at("ident", [P, P], F32)
        top = here[0]

        fg, _ = at("fg", [P, L], F32)
        sn, _ = at("sn", [P, L], F32)
        qx, _ = at("qx", [P, 2, SEQ], F32)
        qt, qr = qx[:, 0, :], qx[:, 1, :]
        vt, _ = at("vt", [P, L], F32)
        gt, _ = at("gt", [P, SEQ], F32)
        gs, _ = at("gs", [P, HALF], F32)
        kt, _ = at("kt", [P, L], F32)
        tree, _ = at("tree", [P, L], F32)
        vv, _ = at("vv", [P, SEQ], F32)
        vm, _ = at("vm", [META, P], F32)
        km, _ = at("km", [META, P], F32)
        st, st_at = at("st", [P, SEQ], F32)
        on, _ = at("on", [P, SEQ], F32, st_at)
        prod, prod_at = at("prod", [P, HALF], F32)
        mask1, _ = at("mask1", [P, MASKS, 64], F32, prod_at)
        mask, _ = at("mask", [P, MASKS, HALF], U8)
        gm, _ = at("gm", [P, 2, HALF], F32)
        assert here[0] <= 229368, here[0]
        last = 4 * (NK - 1) * SEQ
        att, _ = at("att", [P, SEQ], F32, a_hi_at + last)
        ek, _ = at("ek", [P, SEQ], F32, a_lo_at + last)
        xin, _ = at("xin", [P, 3, D], F32, a_hi_at)
        nw, _ = at("nw", [P, D], F32, a_hi_at + 12288)
        hrow, _ = at("hrow", [P, 2, D], F32, a_hi_at + 16384)
        xsq, _ = at("xsq", [P, D], F32, a_hi_at + 24576)

        here[0] = top
        sm, _ = at("sm", [P, 2, HALF], F32)
        yb, _ = at("yb", [P, 2, HALF], F32)
        part, _ = at("part", [P, 2, HALF], F32)
        here[0] = top
        uu, _ = at("uu", [P, 2, L], F32)
        pool_a, _ = at("pool_a", [P, L], F32)
        pool_b, _ = at("pool_b", [P, L], F32)
        p_hi, _ = at("p_hi", [P, 2, SEQ], F32R)
        p_lo, _ = at("p_lo", [P, 2, SEQ], F32R)
        pg, _ = at("pg", [P, 2, SEQ], F32)
        pgs, _ = at("pgs", [P, HALF], F32)
        mx, _ = at("mx", [P, 2, HALF], F32)
        pw, _ = at("pw", [P, 512], F32)
        pw_hi, _ = at("pw_hi", [P, 512], F32R)
        pw_lo, _ = at("pw_lo", [P, 512], F32R)
        assert here[0] <= 229368, here[0]
        here[0] = top
        yp, yp_at = at("yp", [P, 2, HALF], F32)
        sp_in, _ = at("sp_in", [P, 2, HALF], F32)
        pt_in, _ = at("pt_in", [P, 2, HALF], F32)
        mg, _ = at("mg", [P, 2, HALF], F32)
        wo0_hi, _ = at("wo0_hi", [P, NK, HALF], F32R)
        wo0_lo, _ = at("wo0_lo", [P, NK, HALF], F32R)
        assert here[0] <= 229368, here[0]
        zz, _ = at("zz", [P, CHUNKS, HALF], F32, a_hi_at + 16384)
        z1, _ = at("z1", [P, 2, HALF], F32, a_lo_at + 16384)
        xr, _ = at("xr", [P, 2, HALF], F32, a_lo_at + 20480)
        ob, _ = at("ob", [P, 2, HALF], F32, a_lo_at + 24576)
        fnw, _ = at("fnw", [P, D], F32, a_lo_at + 28672)
        row, _ = at("row", [P, 2, D], F32, yp_at)
        z_ss, _ = at("z_ss", [P, 2, CHUNKS], F32, yp_at + 8192)
        z_ms, _ = at("z_ms", [P, CHUNKS], F32, yp_at + 8320)
        z_rs, _ = at("z_rs", [P, CHUNKS], F32, yp_at + 8352)
        zsq, _ = at("zsq", [P, HALF], F32, yp_at + 8448)
        wo1_hi = a_hi[:, :, :].rearrange("p k t -> p (k t)")[:, 0:NK * HALF].rearrange("p (k n) -> p k n", k=NK)
        wo1_lo = a_lo[:, :, :].rearrange("p k t -> p (k t)")[:, 0:NK * HALF].rearrange("p (k n) -> p k n", k=NK)

        acc = [names.enter_context(nc.psum_tensor(f"acc{n}", [P, HALF], F32)) for n in range(4)]
        lev = names.enter_context(nc.psum_tensor("lev", [P, HALF], F32))
        misc = [names.enter_context(nc.psum_tensor(f"misc{n}", [P, HALF], F32)) for n in range(2)]
        small = names.enter_context(nc.psum_tensor("small", [P, HALF], F32))
        VM, KM, KVM = slice(128, 256), slice(256, 384), slice(384, 512)
        h_banks = ((misc[0], misc[1]), (lev, small))

        smp_dram = nc.dram_tensor("smp_spill", [NK, 2, P, HALF], F32, kind="Internal").ap()
        part_dram = nc.dram_tensor("part_spill", [NK, 2, P, HALF], F32, kind="Internal").ap()

        raw_loaded = (S["raw_loaded0"], S["raw_loaded1"])
        x_loaded = (S["x_loaded0"], S["x_loaded1"], S["x_loaded2"])
        smp_stored = (S["smp_stored0"], S["smp_stored1"])
        part_stored = (S["part_stored0"], S["part_stored1"])
        spill_loaded = (S["spill_loaded0"], S["spill_loaded1"])
        xr_loaded = (S["xr_loaded0"], S["xr_loaded1"])
        row_stored = (S["row_stored0"], S["row_stored1"])

        def tile_of(i):
            return (META, 0) if i == 0 else (P, META + (i - 1) * P)

        def level_view(t, m, h):
            return t.rearrange("p (b h j) -> p b h j", h=2, j=1 << m)[:, :, h, :]

        def tree_at(m):
            if m == 0:
                return fg[:, :], META
            lo = sum(L >> n for n in range(1, min(m, 5))) + sum(SEQ >> n for n in range(5, m))
            with_meta = m <= 4
            n = (L if with_meta else SEQ) >> m
            return tree[:, lo:lo + n], (META >> m) if with_meta else 0

        block = names.enter_context(nc.Block())


        @block.sync
        def _(sp):
            sp.dma_start(xin[0:META, 0, :], meta[:, :]).then_inc(x_loaded[0], 16)
            sp.dma_start(xin[:, 1, :], x[0:P, :]).then_inc(x_loaded[1], 16)
            sp.dma_start(xin[:, 2, :], x[P:2 * P, :]).then_inc(x_loaded[2], 16)
            for b in range(2):
                sp.dma_start(raw[:, b, :], wstream[b]).then_inc(raw_loaded[b], 16)
            for i in range(3, CHUNKS + 1):
                sp.wait_ge(S["h_row"], i - 2)
                sp.dma_start(xin[:, i % 3, :], x[(i - 1) * P:i * P, :]).then_inc(x_loaded[i % 3], 16)
            with sp.Fori(1, BLKS // 2) as i:
                for s in range(2):
                    sp.wait_ge(S["w_lo_ready"], i * 2 + (s - 1))
                    sp.dma_start(raw[:, s, :], wstream[i * 2 + s]).then_inc(raw_loaded[s], 16)
            for t in range(CHUNKS):
                sp.wait_ge(S["row_done"], t + 1)
                sp.dma_start(out[t * P:(t + 1) * P, :], row[:, t % 2, :]).then_inc(row_stored[t % 2], 16)
            for s in range(2):
                sp.wait_ge(row_stored[s], 16 * (CHUNKS // 2))

        @block.gpsimd
        def _(pool):
            steps = Steps(pool, S["pool_step"])
            steps.mark(pool.memset(ident[:, :], 0.0))
            steps.mark(pool.memset(minus_half[:, :], -0.5))
            steps.settle()
            pool.affine_select(out=ident[:, :], in_=ident[:, :], compare_op=ALU.not_equal, fill=1.0, base=0,
                               pattern=[[-1, P]], channel_multiplier=1).then_inc(S["consts_made"], 1)

            steps.mark(pool.memset(mask1[:, :, :], 1.0))

            def keep(mask, base, channel, pattern):
                steps.mark(pool.affine_select(out=mask, in_=mask, compare_op=ALU.is_ge, fill=0.0, base=base,
                                              pattern=pattern, channel_multiplier=channel))

            level0 = mask1[:, 0:2, :].rearrange("p a (b j) -> p (a b) j", j=2)
            odd = mask1[:, 3, :]
            halves = [(m, mask1[:, 2 if m == 1 else m + 2, :].rearrange("p (b j) -> p b j", j=1 << m))
                      for m in range(1, 5)]
            steps.settle()
            keep(level0, 0, 1, [[-2, 64], [0, 2]])
            keep(odd, -1, 1, [[-2, 64]])
            for m, view in halves:
                keep(view, 0, 1, [[-(2 << m), 64 >> m], [0, 1 << m]])
            steps.settle()
            keep(level0, 0, -1, [[2, 64], [0, 2]])
            keep(odd, 1, -1, [[2, 64]])
            for m, view in halves:
                ins = pool.affine_select(out=view, in_=view, compare_op=ALU.is_ge, fill=0.0, base=(1 << m) - 1,
                                         pattern=[[2 << m, 64 >> m], [0, 1 << m]], channel_multiplier=-1)
            ins.then_inc(S["masks_made"], 1)

            for i in range(CHUNKS + 1):
                rows = tile_of(i)[0]
                pool.wait_ge(S["x_mean"], i + 1)
                pool.tensor_tensor(x_rs[0:rows, i:i + 1], x_ms[0:rows, i:i + 1], minus_half[0:rows, 0:1],
                                   ALU.pow).then_inc(S["x_rstd"], 1)

            def o_rstd(r):
                pool.wait_ge(S["o_mean"], r + 1)
                pool.tensor_tensor(o_rs[:, :], o_ms[:, :], minus_half[:, 0:CHUNKS], ALU.pow).then_inc(S["o_rstd"], 1)

            with pool.Fori(0, HEADS - 1) as r:
                o_rstd(r)

            def store_smp(n, u):
                for h in range(2):
                    pool.wait_ge(S["acc_read"], u + h + 1)
                    pool.dma_start(smp_dram[n, h], gm[:, h, :]).then_inc(smp_stored[h], 16)

            for n in range(4):
                store_smp(n, first_unit(HEADS) + 2 * n)
            o_rstd(HEADS - 1)
            for n in range(4, NK):
                store_smp(n, U_TAIL + 2 * (n - 4))
            with pool.Fori(0, NK) as n:
                for h in range(2):
                    pool.wait_ge(S["part_made"], n * 2 + (h + 1))
                    pool.dma_start(part_dram[n, h], part[:, h, :]).then_inc(part_stored[h], 16)
            for h in range(2):
                pool.wait_ge(part_stored[h], 16 * NK)
                pool.wait_ge(smp_stored[h], 16 * NK)

            pool.dma_start(pw[:, :], pool_w[0]).then_inc(S["pw_loaded"], 16)
            with pool.Fori(1, 4) as g:
                pool.wait_ge(S["pw_lo_done"], g)
                pool.dma_start(pw[:, :], pool_w[g]).then_inc(S["pw_loaded"], 16)
            pool.wait_ge(S["c_done"], 16)

            def load_spills(n, h):
                pool.dma_start(sp_in[:, h, :], smp_dram[n, h]).then_inc(spill_loaded[h], 16)
                pool.dma_start(pt_in[:, h, :], part_dram[n, h]).then_inc(spill_loaded[h], 16)

            for h in range(2):
                load_spills(0, h)
            with pool.Fori(1, NK) as n:
                for h in range(2):
                    pool.wait_ge(S["merged_done"], n * 2 + (h - 1))
                    load_spills(n, h)
            pool.wait_ge(S["acc_done"], U_OUT)
            pool.dma_start(fnw[:, :], final_norm_w[0:1, :].to_broadcast([P, D])).then_inc(S["fnw_loaded"], 16)

            def residual(v):
                n, t = divmod(v, CHUNKS)
                after(pool, S["z_done"], v - 1)
                pool.dma_start(xr[:, v % 2, :], x[t * P:(t + 1) * P, n * HALF:(n + 1) * HALF]) \
                    .then_inc(xr_loaded[v % 2], 16)

            def z_rstd(t):
                pool.wait_ge(S["z_mean"], t + 1)
                pool.tensor_tensor(z_rs[:, t:t + 1], z_ms[:, t:t + 1], minus_half[:, 0:1], ALU.pow) \
                    .then_inc(S["z_rstd"], 1)

            for v in range(CHUNKS):
                residual(v)
            for v in range(CHUNKS, 2 * CHUNKS):
                residual(v)
                t = v - CHUNKS
                if t:
                    z_rstd(t - 1)
            z_rstd(CHUNKS - 1)

        @block.scalar
        def _(act):
            steps = Steps(act, S["act_step"])
            params = [(bias[:, :, :], b_in[:, :, :]), (logits[:, :, :], lb_logits[:, :, :]), (hgw[:, :], hg_norm_w[:, :]),
                      (psc[:, :], pool_scale[:, :])]
            for dst, src in params:
                act.dma_start(dst, src).then_inc(S["params_loaded"], 16)
            act.dma_start(nw[:, :], norm_w[0:1, :].to_broadcast([P, D])).then_inc(S["norm_row_loaded"], 16)

            def split_hi(b, slot, free, dst=None, left=None):
                if left is not None:
                    act.wait_ge(S["acc_read"], left)
                act.wait_ge(raw_loaded[slot], b * 8 + (16 - 8 * slot))
                after(act, S["acc_done"], free)
                src = raw[:, slot, :] if dst is None else raw[:, slot, :].rearrange("p (k n) -> p k n", k=2)
                act.activation(w_hi[:, slot, :] if dst is None else dst, src, ACT.Copy).then_inc(S["w_hi_ready"], 1)

            def square_x(i):
                rows = tile_of(i)[0]
                act.wait_ge(x_loaded[i % 3], 16 * (i // 3 + 1))
                if i:
                    act.wait_ge(S["x_squared"], i)
                act.activation(xsq[0:rows, :], xin[0:rows, i % 3, :], ACT.Square,
                               accum_out=x_ss[0:rows, i:i + 1]).then_inc(S["x_squared"], 1)

            def h_high(i):
                rows, col = tile_of(i)
                act.wait_ge(S["h_tr"], i + 1)
                for q in range(2):
                    src = h_banks[i % 2][q][:, :].rearrange("p (k t) -> p k t", k=4)[:, :, 0:rows]
                    ins = act.activation(h_hi[:, 4 * q:4 * q + 4, col:col + rows], src, ACT.Copy)
                ins.then_inc(S["h_hi_done"], 1)

            square_x(0)
            split_hi(0, 0, 0)
            square_x(1)
            h_high(0)
            square_x(2)
            h_high(1)
            split_hi(1, 1, 0)
            for i in range(3, CHUNKS + 1):
                square_x(i)
                if i < CHUNKS:
                    h_high(i - 1)

            act.wait_ge(S["params_loaded"], 64)

            def biases(n, before=None, negate=False):
                def copied(row, m, scale):
                    one = ds(m, 1) if not isinstance(m, int) else slice(m, m + 1)
                    steps.mark(act.activation(cur[:, row:row + 1, :], bias[:, one, :], ACT.Copy, scale=scale))

                copied(0, n, 1.0)
                if negate:
                    copied(1, n, -1.0)
                if before is not None:
                    copied(2, before, 1.0)
                steps.settle()

            def leave(u, bank, dst, n, func, part=None, row=0):
                act.wait_ge(S["acc_done"], u + 1)
                b = 0.0 if part is None else cur[:, row, part:part + 1]
                return act.activation(dst, acc[bank][:, 0:n], func, bias=b)

            def leave_f(u, k, bank):
                c0, n = WITH_META[k]
                leave(u, bank, fg[:, c0:c0 + n], n, ACT.Sigmoid, F)
                act.activation(sn[:, c0:c0 + n], acc[bank][:, 0:n], ACT.Sigmoid, bias=cur[:, 1, F:F + 1],
                               scale=-1.0).then_inc(S["acc_read"], 1)

            def leave_v(u, k, bank):
                c0, n = WITH_META[k]
                leave(u, bank, vt[:, c0:c0 + n], n, ACT.Identity, V).then_inc(S["acc_read"], 1)

            def leave_q(u, k, banks):
                leave(u + 6 + k, banks[6 + k], qr[:, k * HALF:(k + 1) * HALF], HALF, ACT.Identity, Q) \
                    .then_inc(S["acc_read"], 1)

            def leave_g(r, u, k):
                after(act, S["a_done"], r * 2)
                after(act, S["gate_done"], r * 2 + k)
                leave(u + 8 + k, BANKS10[8 + k], gt[:, k * HALF:(k + 1) * HALF], HALF, ACT.Identity, G, 2)
                act.activation(gs[:, :], acc[BANKS10[8 + k]][:, :], ACT.Sigmoid, bias=cur[:, 2, G:G + 1]) \
                    .then_inc(S["acc_read"], 1)

            def leave_gm(n, u, banks):
                act.wait_ge(S["acc_read"], u)
                biases(n, HEADS - 1)
                for h in range(2):
                    after(act, smp_stored[h], 16 * n)
                    leave(u + h, banks[h], gm[:, h, :], HALF, ACT.Sigmoid, MP) \
                        .then_inc(S["acc_read"], 1)

            def copy_v(r):
                act.wait_ge(S["v_tr"], r + 1)
                for q in range(2):
                    act.activation(vv[:, q * HALF:(q + 1) * HALF], misc[q][:, :], ACT.Copy)
                act.activation(vm[:, :], small[0:META, VM], ACT.Copy).then_inc(S["v_copied"], 1)

            def copy_k(r):
                act.wait_ge(S["k_tr"], r + 1)
                for q in range(2):
                    act.activation(ek[:, q * HALF:(q + 1) * HALF], misc[q][:, :], ACT.Copy)
                act.activation(km[:, :], small[0:META, KM], ACT.Copy).then_inc(S["k_copied"], 1)

            def square_o(r):
                act.wait_ge(S["o_mm"], r + 1)
                for q in range(2):
                    ins = act.activation(ek[:, q * HALF:(q + 1) * HALF], misc[q][:, :], ACT.Square)
                ins.then_inc(S["o_squared"], 1)

            biases(0, negate=True)
            for k in range(3):
                leave_f(2 * k, k, BANKS8[2 * k])
                leave_v(2 * k + 1, k, BANKS8[2 * k + 1])
                if k == 0:
                    h_high(CHUNKS - 1)
                    h_high(CHUNKS)
                    act.wait_ge(S["lb_shifted"], 1)
                    act.activation(lexp[:, :, :], lexp[:, :, :], ACT.Exp).then_inc(S["lb_exp"], 1)
            split_hi(2, 0, 5)
            split_hi(3, 1, 6)
            for k in range(2):
                leave_q(0, k, BANKS8)
            act.wait_ge(S["masks_made"], 1)
            src = mask1[:, :, :].rearrange("p m (o t) -> p m o t", o=1).to_broadcast([P, MASKS, CHUNKS, 64])
            act.activation(mask[:, :, :].rearrange("p m (c t) -> p m c t", c=CHUNKS), src, ACT.Copy) \
                .then_inc(S["masks_spread"], 1)

            def head_body(j):
                r, u, b = j - 1, first_unit(j), first_block(j)
                copy_v(r)
                split_hi(b + 1, 0, u, left=u)
                biases(j, r, negate=True)
                act.wait_ge(S["level_done"], r * LEVELS + 1)
                for k in range(3):
                    leave_f(u + k, k, BANKS10[k])
                split_hi(b + 2, 1, u + 3)
                for k in range(3):
                    leave_v(u + 3 + k, k, BANKS10[3 + k])
                split_hi(b + 3, 0, u + 6)
                act.wait_ge(S["level_done"], r * LEVELS + 2)
                leave_q(u, 0, BANKS10)
                copy_k(r)
                leave_q(u, 1, BANKS10)
                split_hi(b + 4, 1, u + 8)
                leave_g(r, u, 0)
                square_o(r)
                leave_g(r, u, 1)

            head_body(1)
            with act.Fori(2, HEADS) as j:
                steps.enter(j, 2, 3)
                head_body(j)
            steps.leave(3, HEADS - 2)
            r, u, b = HEADS - 1, first_unit(HEADS), first_block(HEADS)
            copy_v(r)
            for n in range(4):
                split_hi(b + n + 1, (n + b + 1) % 2, u + 2 * n)
                if n < 3:
                    leave_gm(n, u + 2 * n, BANKS10[2 * n:])
            copy_k(r)
            leave_gm(3, u + 6, BANKS10[6:])
            split_hi(b + 5, 0, u + 8)
            leave_g(r, u, 0)
            square_o(r)
            leave_g(r, u, 1)
            for n in range(4):
                split_hi(BLK_TAIL + n + 1, (n + 1) % 2, U_TAIL + 2 * n)
                leave_gm(4 + n, U_TAIL + 2 * n, BANKS8[2 * n:])

            act.wait_ge(S["a_done"], 2 * HEADS)

            def mix_body(n, free):
                b, u = n * 2 + BLK_MIX, n * 4 + U_MIX
                split_hi(b + 1, 1, u, left=u)
                biases(n)
                for h in range(2):
                    after(act, S["part_made"], free + h)
                    leave(u + h, h, sm[:, h, :], HALF, ACT.Sigmoid, MH).then_inc(S["acc_read"], 1)
                split_hi(b + 2, 0, u + 2)
                for h in range(2):
                    leave(u + 2 + h, 2 + h, yb[:, h, :], HALF, ACT.Copy).then_inc(S["acc_read"], 1)

            mix_body(0, -1)
            with act.Fori(1, NK) as n:
                steps.enter(n, 1, 1)
                mix_body(n, n * 2 - 1)
            steps.leave(1, NK - 1)

            for h in range(2):
                act.wait_ge(part_stored[h], 16 * NK)
                act.wait_ge(smp_stored[h], 16 * NK)

            def pool_body(g):
                b, u = g * 4 + BLK_POOL, g * 14 + U_POOL
                split_hi(b + 1, 1, u, left=u)
                biases(g * 2, g * 2 + 1)
                after(act, S["pooled_done"], g * 2)
                for k in range(3):
                    c0, n = WITH_META[k]
                    leave(u + k, BANKS14[k], uu[:, 0, c0:c0 + n], n, ACT.Identity, U) \
                        .then_inc(S["acc_read"], 1)
                split_hi(b + 2, 0, u + 3)
                for k in range(3):
                    c0, n = WITH_META[k]
                    leave(u + 3 + k, BANKS14[3 + k], uu[:, 1, c0:c0 + n], n, ACT.Identity, U, 2) \
                        .then_inc(S["acc_read"], 1)
                split_hi(b + 3, 1, u + 6)
                act.wait_ge(S["pw_loaded"], g * 16 + 16)
                act.activation(pw_hi[:, :], pw[:, :], ACT.Copy).then_inc(S["pw_hi_done"], 1)
                after(act, S["c_done"], g * 4)
                for k in range(4):
                    if k == 2:
                        split_hi(b + 4, 0, u + 8)
                    row = 2 * (k // 2)
                    after(act, S["pgate_done"], g * 4 + k)
                    leave(u + 6 + k, BANKS14[6 + k], pg[:, k // 2, (k % 2) * HALF:(k % 2 + 1) * HALF], HALF,
                          ACT.Identity, PG, row)
                    act.activation(pgs[:, :], acc[BANKS14[6 + k]][:, :], ACT.Sigmoid, bias=cur[:, row, PG:PG + 1]) \
                        .then_inc(S["acc_read"], 1)
                for k in range(4):
                    after(act, S["c_done"], g * 4 + (k - 1))
                    leave(u + 10 + k, BANKS14[10 + k], mx[:, k % 2, :], HALF, ACT.Copy).then_inc(S["acc_read"], 1)

            pool_body(0)
            with act.Fori(1, 4) as g:
                steps.enter(g, 1, 2)
                pool_body(g)
            steps.leave(2, 3)

            act.wait_ge(S["c_done"], 16)

            def down_block(n, bank, split):
                split()
                for h in range(2):
                    after(act, S["merged_done"], n * 2 + (h - 1))
                    leave(n * 2 + (U_DOWN + h), bank + h, yp[:, h, :], HALF, ACT.Copy).then_inc(S["acc_read"], 1)

            down_block(0, 0, lambda: split_hi(BLK_DOWN + 1, 1, U_DOWN))
            down_block(1, 2, lambda: split_hi(BLK_DOWN + 2, 0, U_DOWN + 2))
            with act.Fori(1, NK // 2 - 1) as i:
                for s in range(2):
                    down_block(i * 2 + s, 2 * s,
                               lambda: split_hi(i * 2 + (BLK_DOWN + s + 1), 1 - s, i * 4 + (U_DOWN + 2 * s)))

            def split_out(q):
                split_hi(BLK_OUT + q, q % 2, 0, wo0_hi[:, 2 * q:2 * q + 2, :])

            def split_last():
                split_hi(BLK_OUT - 1, 1, U_OUT - 4)
                split_out(0)
                split_out(1)

            def split_rest():
                split_out(2)
                split_out(3)

            down_block(NK - 2, 0, split_last)
            down_block(NK - 1, 2, split_rest)

            def square_z(v):
                n, t = divmod(v, CHUNKS)
                act.wait_ge(S["z_done"], v + 1)
                if v:
                    act.wait_ge(S["z_squared"], v)
                src = zz[:, t, :] if n == 0 else z1[:, t % 2, :]
                act.activation(zsq[:, :], src, ACT.Square, accum_out=z_ss[:, n, t:t + 1]).then_inc(S["z_squared"], 1)

            for q in range(4):
                split_hi(BLK_OUT + 4 + q, q % 2, U_OUT, wo1_hi[:, 2 * q:2 * q + 2, :])
            act.wait_ge(S["merged_done"], 2 * NK)
            for v in range(2 * CHUNKS):
                after(act, S["z_done"], v - 1)
                leave(U_OUT + v, v % 4, ob[:, v % 2, :], HALF, ACT.Copy).then_inc(S["acc_read"], 1)
                if v:
                    square_z(v - 1)
            square_z(2 * CHUNKS - 1)

        @block.tensor
        def _(pe):
            def three(out_ap, lhs, rhs, first, final):
                pairs = ((lhs[0], rhs[0]), (lhs[0], rhs[1]), (lhs[1], rhs[0]))
                for n, (a, b) in enumerate(pairs):
                    ins = pe.matmul(out_ap, a, b, start=first and n == 0, stop=final and n == 2)
                return ins

            def half_unit(u, bank, slot, rhs, cols, part, late=None):
                c0, n = cols
                if part == 0:
                    after(pe, S["acc_read"], u - 2)
                for k in range(4 * part, 4 * part + 4):
                    if late is not None and k == late[0]:
                        pe.wait_ge(late[1], late[2])
                    w = slice(k * P, (k + 1) * P)
                    ins = three(acc[bank][:, 0:n], (w_hi[:, slot, w], w_lo[:, slot, w]),
                                (rhs[0][:, k, c0:c0 + n], rhs[1][:, k, c0:c0 + n]), k == 0, k == NK - 1)
                if part == 1:
                    ins.then_inc(S["acc_done"], 1)

            def unit(u, bank, slot, rhs, cols):
                for part in range(2):
                    half_unit(u, bank, slot, rhs, cols, part)

            def weights(b):
                pe.wait_ge(S["w_lo_ready"], b + 1)

            def h_transposes(i):
                rows = tile_of(i)[0]
                pe.wait_ge(S["h_row"], i + 1)
                after(pe, S["h_lo_done"], i - 1)
                for k in range(NK):
                    o = (k % 4) * P
                    ins = pe.transpose(h_banks[i % 2][k // 4][:, o:o + rows], hrow[0:rows, i % 2, k * P:(k + 1) * P],
                                       ident[0:rows, 0:rows])
                ins.then_inc(S["h_tr"], 1)

            def v_transposes(r):
                pe.wait_ge(S["acc_read"], first_unit(r) + 6)
                after(pe, S["o_normed"], r)
                for c in range(CHUNKS):
                    pe.transpose(misc[c // 4][:, (c % 4) * P:(c % 4 + 1) * P],
                                 vt[:, META + c * P:META + (c + 1) * P], ident[:, :])
                pe.transpose(small[0:META, VM], vt[:, 0:META], ident[:, :]).then_inc(S["v_tr"], 1)

            def level(r, m):
                if m:
                    pe.wait_ge(S["level_done"], r * LEVELS + m)
                else:
                    pe.wait_ge(S["prepared"], r + 1)
                    pe.wait_ge(S["v_copied"], r + 1)
                for c in range(CHUNKS):
                    s, ks = slice(c * P, (c + 1) * P), slice(META + c * P, META + (c + 1) * P)
                    if m < 2:
                        q = ek[:, s] if m == 0 else \
                            qx[:, :, s].rearrange("p a (b h j) -> p a b h j", h=2, j=2)[:, :, :, 1, :]
                        ins = pe.matmul((lev, small)[c // 4][:, (c % 4) * P:(c % 4 + 1) * P], kt[:, ks], q,
                                        start=True, stop=True)
                        continue
                    halves = 1 if m != LEVELS - 2 else 2
                    rows, n = (P if m < LEVELS - 2 else 1 << m), 64 // halves
                    q = level_view(qt[:, s], m, 1)
                    for h in range(halves):
                        s0, o = h * (2 << m), c * 64 + h * n
                        ins = pe.matmul(lev[s0:s0 + rows, o:o + n], kt[:, META + c * P + s0:META + c * P + s0 + rows],
                                        q if halves == 1 else q[:, h, :], start=True, stop=True)
                ins.then_inc(S["level_mm"], 1)

            def k_transposes(r):
                pe.wait_ge(S["level_done"], r * LEVELS + LEVELS)
                after(pe, S["a_done"], r * 2)
                for c in range(CHUNKS):
                    pe.transpose(misc[c // 4][:, (c % 4) * P:(c % 4 + 1) * P],
                                 kt[:, META + c * P:META + (c + 1) * P], ident[:, :])
                pe.transpose(small[0:META, KM], kt[:, 0:META], ident[:, :]).then_inc(S["k_tr"], 1)

            def k_times_v(r):
                pe.wait_ge(S["k_copied"], r + 1)
                pe.matmul(small[:, KVM], km[:, :], vm[:, :], start=True, stop=True)
                for c in range(CHUNKS - 1):
                    s = slice(c * P, (c + 1) * P)
                    ins = pe.matmul(misc[c // 4][:, (c % 4) * P:(c % 4 + 1) * P], ek[:, s], vv[:, s],
                                    start=True, stop=True)
                ins.then_inc(S["kv_mm"], 1)

            def outputs(r):
                pe.wait_ge(S["state_done"], r + 1)
                for c in range(CHUNKS):
                    s = slice(c * P, (c + 1) * P)
                    dst = misc[c // 4][:, (c % 4) * P:(c % 4 + 1) * P]
                    pe.matmul(dst, qt[:, s], st[:, s], start=True, stop=False)
                    ins = pe.matmul(dst, att[:, s], vv[:, s], start=False, stop=True)
                ins.then_inc(S["o_mm"], 1)

            def o_transposes(r, v_next):
                pe.wait_ge(S["o_normed"], r + 1)
                if v_next:
                    pe.wait_ge(S["v_copied"], r + 2)
                for c in range(CHUNKS):
                    ins = pe.transpose(misc[c // 4][:, (c % 4) * P:(c % 4 + 1) * P], on[:, c * P:(c + 1) * P],
                                       ident[:, :])
                ins.then_inc(S["o_tr"], 1)

            def stage(pos, r, o_before):
                if pos == 0:
                    v_transposes(r)
                elif pos in LEVEL_AT:
                    level(r, LEVEL_AT.index(pos))
                elif pos == 3 and o_before:
                    o_transposes(r - 1, True)
                elif pos == 15:
                    k_transposes(r)
                elif pos == 16:
                    k_times_v(r)
                elif pos == 18:
                    outputs(r)

            hs, aa = (h_hi, h_lo), (a_hi, a_lo)
            head_blocks = ((0, WITH_META), (3, WITH_META), (6, NO_META), (8, NO_META))
            pe.wait_ge(S["consts_made"], 1)
            for k, cols in enumerate(WITH_META):
                for i in ((0, 1, 2, 3), (4, 5, 6), (7, 8))[k]:
                    h_transposes(i)
                pe.wait_ge(S["h_lo_done"], (4, 7, 9)[k])
                for blk in range(2):
                    if k == 0:
                        weights(blk)
                    unit(2 * k + blk, BANKS8[2 * k + blk], blk, hs, cols)
            weights(2)
            for k, cols in enumerate(NO_META):
                unit(6 + k, BANKS8[6 + k], 0, hs, cols)

            def head_body(j, o_before):
                u, b = first_unit(j), first_block(j)
                for blk, (u0, cols) in enumerate(head_blocks):
                    for k, c in enumerate(cols):
                        for part in range(2):
                            stage(2 * (u0 + k) + part, j - 1, o_before)
                            if k == 0 and part == 0:
                                weights(b + blk)
                            half_unit(u + (u0 + k), BANKS10[u0 + k], (blk + 1) % 2, hs, c, part)

            head_body(1, False)
            with pe.Fori(2, HEADS) as j:
                head_body(j, True)
            u, b = first_unit(HEADS), first_block(HEADS)
            for k in range(10):
                for part in range(2):
                    stage(2 * k + part, HEADS - 1, True)
                    if k % 2 == 0 and part == 0:
                        weights(b + k // 2)
                    half_unit(u + k, BANKS10[k], (k // 2 + 1) % 2, hs, NO_META[k % 2], part)
            for k in range(8):
                if k % 2 == 0:
                    weights(BLK_TAIL + k // 2)
                unit(U_TAIL + k, BANKS8[k], (k // 2) % 2, hs, NO_META[k % 2])
                if k == 0:
                    o_transposes(HEADS - 1, False)

            pe.wait_ge(S["a_done"], 2 * HEADS)
            with pe.Fori(0, NK) as n:
                weights(n * 2 + BLK_MIX)
                for h in range(2):
                    unit(n * 4 + (U_MIX + h), h, 0, hs, NO_META[h])
                weights(n * 2 + (BLK_MIX + 1))
                for h in range(2):
                    unit(n * 4 + (U_MIX + 2 + h), 2 + h, 1, aa, (h * HALF, HALF))

            with pe.Fori(0, 4) as g:
                u, b = g * 14 + U_POOL, g * 4 + BLK_POOL
                for blk, (u0, cols) in enumerate(((0, WITH_META), (3, WITH_META), (6, NO_META), (8, NO_META))):
                    weights(b + blk)
                    for k, c in enumerate(cols):
                        unit(u + (u0 + k), BANKS14[u0 + k], blk % 2, hs, c)
                pe.wait_ge(S["pooled_done"], g * 2 + 2)
                pe.wait_ge(S["pw_lo_done"], g + 1)
                for k in range(4):
                    o, c0 = k // 2, (k % 2) * HALF
                    pe.wait_ge(S["acc_read"], u + (8 + k))
                    for i in range(2):
                        w = slice(i * 256 + o * P, i * 256 + (o + 1) * P)
                        ins = three(acc[BANKS14[10 + k]][:, :], (pw_hi[:, w], pw_lo[:, w]),
                                    (p_hi[:, i, c0:c0 + HALF], p_lo[:, i, c0:c0 + HALF]), i == 0, i == 1)
                    ins.then_inc(S["acc_done"], 1)

            pe.wait_ge(S["c_done"], 12)
            with pe.Fori(0, NK // 2) as i:
                for s in range(2):
                    weights(i * 2 + (BLK_DOWN + s))
                    for h in range(2):
                        for part in range(2):
                            half_unit(i * 4 + (U_DOWN + 2 * s + h), 2 * s + h, s, aa, (h * HALF, HALF), part,
                                      (6, S["c_done"], 16))

            pe.wait_ge(S["merged_done"], 2 * NK - 2)
            for n, wo in enumerate(((wo0_hi, wo0_lo), (wo1_hi, wo1_lo))):
                for t in range(CHUNKS):
                    v = n * CHUNKS + t
                    pe.wait_ge(S["acc_read"], U_OUT + v - 2)
                    s = slice(META + t * P, META + (t + 1) * P)
                    for k in range(NK):
                        if t == 0 and k % 2 == 0:
                            weights(BLK_OUT + 4 * n + k // 2)
                        if v in (0, 4) and k == NK - 1:
                            pe.wait_ge(S["merged_done"], 2 * NK - 1 + v // 4)
                        ins = three(acc[v % 4][:, :], (h_hi[:, k, s], h_lo[:, k, s]), (wo[0][:, k, :], wo[1][:, k, :]),
                                    k == 0, k == NK - 1)
                    ins.then_inc(S["acc_done"], 1)

        @block.vector
        def _(dve):
            steps = Steps(dve, S["vec_step"])
            steps.mark(dve.memset(att[:, :], 0.0))
            def x_mean(i):
                rows = tile_of(i)[0]
                dve.wait_ge(S["x_squared"], i + 1)
                dve.tensor_scalar(x_ms[0:rows, i:i + 1], x_ss[0:rows, i:i + 1], 1.0 / D, EPS, ALU.mult, ALU.add) \
                    .then_inc(S["x_mean"], 1)

            def h_row(i):
                rows = tile_of(i)[0]
                dve.wait_ge(S["x_rstd"], i + 1)
                after(dve, S["h_tr"], i - 1)
                dve.scalar_tensor_tensor(hrow[0:rows, i % 2, :], xin[0:rows, i % 3, :], x_rs[0:rows, i:i + 1],
                                         nw[0:rows, :], ALU.mult, ALU.mult).then_inc(S["h_row"], 1)

            def h_low(i):
                rows, col = tile_of(i)
                dve.wait_ge(S["h_hi_done"], i + 1)
                for q in range(2):
                    src = h_banks[i % 2][q][:, :].rearrange("p (k t) -> p k t", k=4)[:, :, 0:rows]
                    ks, ts = slice(4 * q, 4 * q + 4), slice(col, col + rows)
                    ins = dve.tensor_tensor(h_lo[:, ks, ts], src, h_hi[:, ks, ts].bitcast(F32), ALU.subtract)
                ins.then_inc(S["h_lo_done"], 1)

            def split_lo(b, slot, dst=None, hi=None):
                dve.wait_ge(S["w_hi_ready"], b + 1)
                src = raw[:, slot, :]
                if dst is None:
                    dst, hi = w_lo[:, slot, :], w_hi[:, slot, :]
                else:
                    src = src.rearrange("p (k n) -> p k n", k=2)
                dve.tensor_tensor(dst, src, hi.bitcast(F32), ALU.subtract).then_inc(S["w_lo_ready"], 1)

            x_mean(0)
            dve.wait_ge(S["norm_row_loaded"], 16)
            for i in range(CHUNKS + 1):
                h_row(i)
                if i < CHUNKS:
                    x_mean(i + 1)
                if i == 1:
                    split_lo(0, 0)
                if i:
                    h_low(i - 1)
                if i == 3:
                    split_lo(1, 1)
            h_low(CHUNKS)
            dve.wait_ge(S["params_loaded"], 64)
            steps.mark(dve.tensor_tensor(lmax[:, :], logits[:, 0, :], logits[:, 1, :], ALU.max))
            steps.settle()
            for n in range(2):
                ins = dve.tensor_tensor(lexp[:, n, :], logits[:, n, :], lmax[:, :], ALU.subtract)
            ins.then_inc(S["lb_shifted"], 1)

            dve.wait_ge(S["lb_exp"], 1)
            steps.mark(dve.tensor_tensor(lmax[:, :], lexp[:, 0, :], lexp[:, 1, :], ALU.add))
            steps.settle()
            steps.mark(dve.reciprocal(lmax[:, :], lmax[:, :]))
            steps.settle()
            steps.mark(dve.tensor_tensor(lb[:, :], lexp[:, 0, :], lmax[:, :], ALU.mult))
            steps.settle()
            steps.mark(dve.tensor_scalar(one_minus_lb[:, :], lb[:, :], -1.0, 1.0, ALU.mult, ALU.add))

            def prepare_gates(r, u):
                dve.wait_ge(S["acc_read"], u)
                one = ds(r, 1)
                steps.mark(dve.tensor_scalar(kt[:, :], sn[:, :], one_minus_lb[:, one], None, ALU.mult))
                steps.mark(dve.tensor_scalar(fg[:, :], fg[:, :], one_minus_lb[:, one], lb[:, one], ALU.mult, ALU.add))

            def prepare(r):
                dve.wait_ge(S["acc_read"], first_unit(r) + 8)
                steps.settle()
                even, odd = level_view(ek[:, :], 0, 0), level_view(ek[:, :], 0, 1)
                steps.mark(dve.tensor_tensor(qt, qr, fg[:, META:L], ALU.mult))
                steps.mark(dve.tensor_copy(even, level_view(qr, 0, 0)))
                steps.settle()
                dve.tensor_copy(odd, level_view(qt, 0, 1))
                fours = qr.rearrange("p (b j) -> p b j", j=4)
                dve.tensor_copy(fours[:, :, 2:3], fours[:, :, 1:2]).then_inc(S["prepared"], 1)

            def entries(m, scale_k):
                if m != 1:
                    scale_k()
                if m < 2:
                    for q, bank in enumerate((lev, small)):
                        s = slice(q * HALF, (q + 1) * HALF)
                        a, p = att[:, s], bank[:, :]
                        if m == 0:
                            keep = mask[:, 0:2, 0:256].rearrange("p a (c t) -> p c a t", t=64)
                            steps.mark(dve.copy_predicated(a.rearrange("p (c a t) -> p c a t", a=2, t=64), keep,
                                                           p.rearrange("p (c a t) -> p c a t", a=2, t=64)))
                            continue
                        p = p.rearrange("p (c a t) -> p c a t", a=2, t=64)
                        keep = mask[:, 2:4, 0:256].rearrange("p a (c t) -> p a c t", t=64)
                        fours = a.rearrange("p (c b h j) -> p c b h j", b=32, h=2, j=2)[:, :, :, 1, :]
                        steps.mark(dve.copy_predicated(fours, keep[:, 0].rearrange("p c (b j) -> p c b j", j=2),
                                                       p[:, :, 0, :].rearrange("p c (b j) -> p c b j", j=2)))
                    if m == 1:
                        steps.settle()
                        scale_k()
                        for q, bank in enumerate((lev, small)):
                            p = bank[:, :].rearrange("p (c a t) -> p c a t", a=2, t=64)
                            odd = att[:, q * HALF:(q + 1) * HALF].rearrange("p (c t h) -> p c t h", t=64, h=2)
                            keep = mask[:, 3, 0:256].rearrange("p (c t) -> p c t", t=64)
                            steps.mark(dve.copy_predicated(odd[:, :, :, 1], keep, p[:, :, 1, :]))
                    return
                a, p = level_view(att[:, :], m, 1), lev[:, :].rearrange("p (b j) -> p b j", j=1 << m)
                if m < LEVELS - 2:
                    keep = mask[:, m + 2, :].rearrange("p (b j) -> p b j", j=1 << m)
                    steps.mark(dve.copy_predicated(a, keep, p))
                    return
                for h in range(1 if m == LEVELS - 1 else 2):
                    rows = slice(h * (2 << m), h * (2 << m) + (1 << m))
                    if m == LEVELS - 2:
                        ah, ph = (v.rearrange("p (c g) j -> p c g j", g=2)[rows, :, h, :] for v in (a, p))
                    else:
                        ah, ph = a[rows], p[rows]
                    steps.mark(dve.tensor_copy(ah, ph))

            def level(r, m):
                now, x0 = tree_at(m)
                up, _ = tree_at(m + 1)
                pairs = now if m <= 3 else now[:, x0:]
                pairs = pairs.rearrange("p (b h) -> p b h", h=2)
                dve.wait_ge(S["level_mm"], r * LEVELS + m + 1)
                steps.mark(dve.tensor_tensor(up, pairs[:, :, 0], pairs[:, :, 1], ALU.mult))
                j = 1 << m
                keys = kt[:, :] if m <= 3 else kt[:, META:L]
                nb = (L if m <= 3 else SEQ) >> (m + 1)
                ks = level_view(keys, m, 0)
                entries(m, lambda: dve.tensor_tensor(ks, ks, pairs[:, :, 1:2].to_broadcast([P, nb, j]), ALU.mult))
                queries = now[:, x0:].rearrange("p (b h) -> p b h", h=2)
                qs = level_view(qt, m, 1)
                dve.tensor_tensor(qs, qs, queries[:, :, 0:1].to_broadcast([P, SEQ >> (m + 1), j]), ALU.mult) \
                    .then_inc(S["level_done"], 1)
                steps.settle()

            def states(r):
                dve.wait_ge(S["kv_mm"], r + 1)
                decay, _ = tree_at(LEVELS)
                steps.mark(dve.tensor_copy(st[:, 0:P], small[:, KVM]))
                for c in range(CHUNKS - 1):
                    steps.settle()
                    ins = dve.scalar_tensor_tensor(st[:, (c + 1) * P:(c + 2) * P], st[:, c * P:(c + 1) * P],
                                                   decay[:, c:c + 1], misc[c // 4][:, (c % 4) * P:(c % 4 + 1) * P],
                                                   ALU.mult, ALU.add)
                    if c < CHUNKS - 2:
                        steps.mark(ins)
                ins.then_inc(S["state_done"], 1)

            def normalise_o(r):
                dve.wait_ge(S["o_squared"], r + 1)
                steps.mark(dve.tensor_reduce(o_ss[:, :], ek[:, :].rearrange("p (c d) -> p c d", d=P), AX.X, ALU.add))
                steps.settle()
                dve.tensor_scalar(o_ms[:, :], o_ss[:, :], 1.0 / P, EPS, ALU.mult, ALU.add).then_inc(S["o_mean"], 1)
                dve.wait_ge(S["o_rstd"], r + 1)
                for q in range(2):
                    rs = o_rs[:, 4 * q:4 * q + 4].rearrange("p (c o) -> p c o", o=1).to_broadcast([P, 4, P])
                    ins = dve.tensor_tensor(on[:, q * HALF:(q + 1) * HALF].rearrange("p (c d) -> p c d", d=P),
                                            misc[q][:, :].rearrange("p (c d) -> p c d", d=P), rs, ALU.mult)
                ins.then_inc(S["o_normed"], 1)

            def gate(r, u, k):
                dve.wait_ge(S["acc_read"], u + (9 + k))
                g = gt[:, k * HALF:(k + 1) * HALF]
                dve.scalar_tensor_tensor(g, g, hgw[:, ds(r, 1)], gs[:, :], ALU.mult, ALU.mult) \
                    .then_inc(S["gate_done"], 1)

            def gated_o(r):
                dve.wait_ge(S["gate_done"], r * 2 + 2)
                dve.wait_ge(S["o_tr"], r + 1)
                for q in range(2):
                    s = slice(q * HALF, (q + 1) * HALF)
                    o = misc[q][:, :].rearrange("p (o t) -> p o t", o=1)
                    g = gt[:, s].rearrange("p (o t) -> p o t", o=1)
                    pr = prod[:, :].rearrange("p (o t) -> p o t", o=1)
                    after(dve, S["a_done"], r * 2 + q)
                    dve.tensor_tensor(a_hi[:, ds(r, 1), s], o, g, ALU.mult)
                    steps.mark(dve.tensor_tensor(pr, o, g, ALU.mult))
                    steps.settle()
                    dve.tensor_tensor(a_lo[:, ds(r, 1), s], pr, a_hi[:, ds(r, 1), s].bitcast(F32), ALU.subtract) \
                        .then_inc(S["a_done"], 1)

            split_lo(2, 0)
            split_lo(3, 1)
            steps.settle()
            prepare_gates(0, 6)

            def head_body(j, o_before):
                r, u, b = j - 1, first_unit(j), first_block(j)
                prepare(r)
                split_lo(b + 1, 0)
                level(r, 0)
                if o_before:
                    gated_o(r - 1)
                level(r, 1)
                level(r, 2)
                split_lo(b + 2, 1)
                level(r, 3)
                level(r, 4)
                level(r, 5)
                split_lo(b + 3, 0)
                level(r, 6)
                states(r)
                prepare_gates(j, u + 3)
                split_lo(b + 4, 1)
                gate(r, u, 0)
                normalise_o(r)
                gate(r, u, 1)

            PER_HEAD = 4 + 2 * LEVELS + (1 + 3 + 1) + (CHUNKS - 1) + 1 + 2
            dve.wait_ge(S["masks_spread"], 1)
            head_body(1, False)
            with dve.Fori(2, HEADS) as j:
                steps.enter(j, 2, PER_HEAD)
                head_body(j, True)
            steps.leave(PER_HEAD, HEADS - 2)
            r, u, b = HEADS - 1, first_unit(HEADS), first_block(HEADS)
            prepare(r)
            split_lo(b + 1, 0)
            level(r, 0)
            gated_o(r - 1)
            level(r, 1)
            split_lo(b + 2, 1)
            level(r, 2)
            level(r, 3)
            split_lo(b + 3, 0)
            level(r, 4)
            level(r, 5)
            split_lo(b + 4, 1)
            level(r, 6)
            states(r)
            split_lo(b + 5, 0)
            gate(r, u, 0)
            normalise_o(r)
            gate(r, u, 1)
            split_lo(BLK_TAIL + 1, 1)
            gated_o(r)
            for n in range(2, 5):
                split_lo(BLK_TAIL + n, n % 2)

            def mix_body(n, stored):
                b, u = n * 2 + BLK_MIX, n * 4 + U_MIX
                split_lo(b + 1, 1)
                split_lo(b + 2, 0)
                for h in range(2):
                    dve.wait_ge(S["acc_read"], u + (3 + h))
                    after(dve, part_stored[h], stored)
                    dve.tensor_tensor(part[:, h, :], sm[:, h, :], yb[:, h, :], ALU.mult).then_inc(S["part_made"], 1)

            mix_body(0, 0)
            with dve.Fori(1, NK) as n:
                mix_body(n, n * 16)

            def pooled(g, k, u):
                w, src = WINDOWS[g], uu[:, k, :]
                dve.wait_ge(S["acc_read"], u + 3 * (k + 1))
                after(dve, S["pooled_done"], 2 * g + k)
                after(dve, S["c_done"], 4 * g)
                bufs, s = [pool_a, pool_b], src
                for n in range(w.bit_length() - 1):
                    lo, step = (2 << n) - 1, 1 << n
                    dst = bufs[n % 2][:, :]
                    steps.mark(dve.tensor_tensor(dst[:, lo:L], s[:, lo:L], s[:, lo - step:L - step], ALU.add))
                    steps.settle()
                    s = dst
                tmp = bufs[(w.bit_length() - 1) % 2][:, META:L]
                dve.scalar_tensor_tensor(p_hi[:, k, :], s[:, META:L], 1.0 / w, src[:, META:L], ALU.mult, ALU.subtract)
                steps.mark(dve.scalar_tensor_tensor(tmp, s[:, META:L], 1.0 / w, src[:, META:L], ALU.mult,
                                                    ALU.subtract))
                steps.settle()
                dve.tensor_tensor(p_lo[:, k, :], tmp, p_hi[:, k, :].bitcast(F32), ALU.subtract) \
                    .then_inc(S["pooled_done"], 1)

            def pool_gate(g, k, u):
                dve.wait_ge(S["acc_read"], u + 7 + k)
                v = pg[:, k // 2, (k % 2) * HALF:(k % 2 + 1) * HALF]
                n = 2 * g + k // 2
                dve.scalar_tensor_tensor(v, v, psc[:, n:n + 1], pgs[:, :], ALU.mult, ALU.mult) \
                    .then_inc(S["pgate_done"], 1)

            for g in range(4):
                b, u = BLK_POOL + 4 * g, U_POOL + 14 * g
                split_lo(b + 1, 1)
                split_lo(b + 2, 0)
                pooled(g, 0, u)
                split_lo(b + 3, 1)
                pooled(g, 1, u)
                dve.wait_ge(S["pw_hi_done"], g + 1)
                dve.tensor_tensor(pw_lo[:, :], pw[:, :], pw_hi[:, :].bitcast(F32), ALU.subtract) \
                    .then_inc(S["pw_lo_done"], 1)
                pool_gate(g, 0, u)
                pool_gate(g, 1, u)
                split_lo(b + 4, 0)
                pool_gate(g, 2, u)
                pool_gate(g, 3, u)
                dve.wait_ge(S["pgate_done"], 4 * g + 4)
                for k in range(4):
                    n, s = 2 * g + k // 2, slice((k % 2) * HALF, (k % 2 + 1) * HALF)
                    dve.wait_ge(S["acc_read"], u + 11 + k)
                    after(dve, S["c_done"], 4 * g + k)
                    dve.wait_ge(S["pooled_done"], 2 * g + 2)
                    tmp = pool_a[:, 0:HALF]
                    dve.tensor_tensor(a_hi[:, n, s], mx[:, k % 2, :], pg[:, k // 2, s], ALU.mult)
                    steps.mark(dve.tensor_tensor(tmp, mx[:, k % 2, :], pg[:, k // 2, s], ALU.mult))
                    steps.settle()
                    dve.tensor_tensor(a_lo[:, n, s], tmp, a_hi[:, n, s].bitcast(F32), ALU.subtract) \
                        .then_inc(S["c_done"], 1)

            def merge(n, h):
                dve.wait_ge(S["acc_read"], n * 2 + (U_DOWN + h + 1))
                dve.wait_ge(spill_loaded[h], n * 32 + 32)
                s = slice(META + h * HALF, META + (h + 1) * HALF)
                one, hh = ds(n, 1), slice(h, h + 1)
                steps.mark(dve.tensor_tensor(mg[:, hh, :], yp[:, hh, :], sp_in[:, hh, :], ALU.mult))
                steps.settle()
                dve.tensor_tensor(h_hi[:, one, s], mg[:, hh, :], pt_in[:, hh, :], ALU.add)
                steps.mark(dve.tensor_tensor(mg[:, hh, :], mg[:, hh, :], pt_in[:, hh, :], ALU.add))
                steps.settle()
                dve.tensor_tensor(h_lo[:, one, s], mg[:, hh, :], h_hi[:, one, s].bitcast(F32), ALU.subtract) \
                    .then_inc(S["merged_done"], 1)

            PER_PAIR = 8
            with dve.Fori(0, NK // 2 - 1) as i:
                steps.enter(i, 0, PER_PAIR)
                for s in range(2):
                    split_lo(i * 2 + (BLK_DOWN + s + 1), 1 - s)
                    for h in range(2):
                        merge(i * 2 + s, h)
            steps.leave(PER_PAIR, NK // 2 - 1)
            split_lo(BLK_OUT - 1, 1)
            for n in range(NK - 2, NK):
                for q in range(2 * (n - NK + 2), 2 * (n - NK + 3)):
                    ks = slice(2 * q, 2 * q + 2)
                    split_lo(BLK_OUT + q, q % 2, wo0_lo[:, ks, :], wo0_hi[:, ks, :])
                for h in range(2):
                    merge(n, h)
            for q in range(4):
                ks = slice(2 * q, 2 * q + 2)
                split_lo(BLK_OUT + 4 + q, q % 2, wo1_lo[:, ks, :], wo1_hi[:, ks, :])

            def z_of(v):
                n, t = divmod(v, CHUNKS)
                return zz[:, t, :] if n == 0 else z1[:, t % 2, :]

            def add_residual(v):
                dve.wait_ge(S["acc_read"], U_OUT + v + 1)
                dve.wait_ge(xr_loaded[v % 2], 16 * (v // 2 + 1))
                after(dve, S["row_done"], v - CHUNKS - 1)
                dve.tensor_tensor(z_of(v), ob[:, v % 2, :], xr[:, v % 2, :], ALU.add).then_inc(S["z_done"], 1)

            def finish_rows(t):
                dve.wait_ge(S["z_squared"], CHUNKS + t + 1)
                one = slice(t, t + 1)
                steps.mark(dve.tensor_tensor(z_ms[:, one], z_ss[:, 0, one], z_ss[:, 1, one], ALU.add))
                steps.settle()
                dve.tensor_scalar(z_ms[:, one], z_ms[:, one], 1.0 / D, EPS, ALU.mult, ALU.add) \
                    .then_inc(S["z_mean"], 1)
                dve.wait_ge(S["z_rstd"], t + 1)
                after(dve, row_stored[t % 2], 16 * (t // 2))
                for n in range(2):
                    s = slice(n * HALF, (n + 1) * HALF)
                    ins = dve.scalar_tensor_tensor(row[:, t % 2, s], z_of(n * CHUNKS + t), z_rs[:, one], fnw[:, s],
                                                   ALU.mult, ALU.mult)
                ins.then_inc(S["row_done"], 1)

            for v in range(CHUNKS + 1):
                add_residual(v)
            dve.wait_ge(S["fnw_loaded"], 16)
            for v in range(CHUNKS + 1, 2 * CHUNKS):
                finish = v - CHUNKS - 1
                add_residual(v)
                finish_rows(finish)
            finish_rows(CHUNKS - 1)


def kernel(**inputs):
    import numpy as np
    import concourse.bacc as bacc
    from concourse.bass_utils import run_bass_kernel_spmd

    def blocks(w):
        r, c = w.shape
        return w.reshape(r // P, P, c // P, P).transpose(2, 1, 0, 3).reshape(c // P, P, r)

    mats = {"in": blocks(inputs["w_in"][0]), "down_hg": blocks(inputs["w_down_hg"][0]),
            "down_pool": blocks(inputs["w_down_pool"][0])}
    mats["out"] = inputs["w_out"][0].reshape(4, 2, P, 2, HALF).transpose(3, 0, 2, 1, 4).reshape(8, P, D)
    arrays = {
        "x": inputs["x"][0],
        "meta": inputs["meta_tokens"],
        "norm_w": inputs["norm_w"],
        "wstream": np.stack([mats[m][n] for m, n in stream_order()]),
        "pool_w": inputs["pool_w"][0].reshape(4, 2, P, 256).transpose(0, 2, 1, 3).reshape(4, P, 512),
        "b_in": inputs["b_in"][0].reshape(8, 8, P).transpose(2, 1, 0),
        "lb_logits": inputs["lb_logits"].reshape(2, HEADS, P).transpose(2, 0, 1),
        "hg_norm_w": inputs["hg_norm_w"][0].reshape(HEADS, P).T,
        "pool_scale": inputs["pool_scale"][0].reshape(NK, P).T,
        "final_norm_w": inputs["final_norm_w"].reshape(1, D),
    }
    nc = bacc.Bacc("TRN2", target_bir_lowering=False, num_devices=1)
    fed, args = {}, {}
    for name, a in arrays.items():
        a = np.ascontiguousarray(a)
        fed[f"in_{name}"] = a
        args[name] = nc.dram_tensor(f"in_{name}", a.shape, mybir.dt.from_np(a.dtype), kind="ExternalInput").ap()
    args["out"] = nc.dram_tensor("out_z", (SEQ, D), F32, kind="ExternalOutput").ap()
    hybrid_block(nc, **args)
    r = run_bass_kernel_spmd(nc, [fed], core_ids=[0])
    return r.results[0]["out_z"].reshape(1, SEQ, D)
```

```python
from contextlib import ExitStack

import concourse.bass as bass
from concourse import mybir

ALU = mybir.AluOpType
ACT = mybir.ActivationFunctionType
AX = mybir.AxisListType
F32 = mybir.dt.float32
F32R = mybir.dt.float32r
U8 = mybir.dt.uint8
ds = bass.ds

P = 128
D = 1024
NK = D // P
SEQ = 1024
META = 16
L = META + SEQ
HEADS = 8
CHUNKS = SEQ // P
LEVELS = 7
STEPS = 6
HALF = 512
WINDOWS = (2, 4, 8, 16)
EPS = 1e-6

Q, F, V, G, U, PG, MH, MP = range(8)

WITH_META = ((0, 348), (348, 346), (694, 346))
NO_META = ((META, HALF), (META + HALF, HALF))
FIRST = ((0, 272), (272, 256), (528, 256), (784, 256))

BLK_TAIL, BLK_MIX, BLK_POOL, BLK_DOWN, BLK_OUT, BLKS = 36, 40, 56, 72, 80, 88
U_TAIL, U_MIX, U_POOL, U_DOWN, U_OUT = 90, 98, 130, 186, 202
MASKS = 8
STEP_AT = (2, 4, 8, 11, 13, 14)
STEP_LEVEL = (0, 1, 2, 4, 5, 6)
WARM_UP = (16, 4, 6, 8)
BANKS8 = (0, 1, 2, 3, 0, 1, 2, 3)
BANKS10 = (0, 1, 2, 0, 1, 2, 0, 1, 2, 3)
BANKS14 = (0, 1, 2, 3, 0, 1, 2, 3, 0, 1, 2, 0, 1, 3)


def stream_order():
    order = []
    for j in range(HEADS):
        order += [("in", 8 * F + j), ("in", 8 * V + j), ("in", 8 * Q + j)]
        if j:
            order.append(("in", 8 * G + j - 1))
    order += [("in", 8 * MP + n) for n in range(4)] + [("in", 8 * G + HEADS - 1)]
    order += [("in", 8 * MP + n) for n in range(4, 8)]
    for n in range(8):
        order += [("in", 8 * MH + n), ("down_hg", n)]
    for g in range(4):
        order += [("in", 8 * U + 2 * g), ("in", 8 * U + 2 * g + 1), ("in", 8 * PG + 2 * g),
                  ("in", 8 * PG + 2 * g + 1)]
    order += [("down_pool", n) for n in range(8)]
    order += [("out", n) for n in range(8)]
    return order


def after(eng, sem, count):
    if not isinstance(count, int) or count > 0:
        eng.wait_ge(sem, count)


def v_read(r):
    return 8 if isinstance(r, int) and r == 0 else r * 10 + 6


def q_read(r):
    return 10 if isinstance(r, int) and r == 0 else r * 10 + 8


def first_block(j):
    return 0 if isinstance(j, int) and j == 0 else j * 4 - 1


class Steps:

    def __init__(self, eng, sem):
        self.eng, self.sem, self.base, self.n = eng, sem, 0, 0

    def mark(self, instruction):
        instruction.then_inc(self.sem, 1)
        self.n += 1

    def settle(self):
        self.eng.wait_ge(self.sem, self.base + self.n)

    def enter(self, i, i0, per):
        self.start = self.base + self.n
        self.base, self.n = (i - i0) * per + self.start, 0

    def leave(self, per, times):
        assert self.n == per, (self.n, per)
        self.base, self.n = self.start + per * times, 0


def hybrid_block(nc, x, meta, norm_w, wstream, pool_w, b_in, lb_logits, hg_norm_w, pool_scale, final_norm_w, out):
    names = ExitStack()
    with names:
        sem_names = [
            "params_loaded", "logits_loaded", "norm_row_loaded", "x_loaded0", "x_loaded1", "x_loaded2",
            "raw_loaded0", "raw_loaded1",
            "lb_shifted", "lb_exp", "consts_made", "masks_made", "masks_spread", "pool_step",
            "x_squared", "x_mean", "x_rstd", "h_row", "h_tr", "h_hi_done", "h_lo_done",
            "w_hi_ready", "w_lo_ready", "acc_done", "acc_read",
            "prepared", "v_tr", "v_copied", "level_mm", "level_done", "k_tr", "k_copied", "kv_mm",
            "state_done", "o_mm", "o_squared", "o_mean", "o_rstd", "o_normed", "o_tr", "a_done", "gate_done",
            "smp_stored0", "smp_stored1", "part_made", "part_stored0", "part_stored1",
            "pooled_done", "pgate_done", "pw_loaded", "pw_hi_done", "pw_lo_done", "c_done",
            "spill_loaded0", "spill_loaded1", "merged_done",
            "fnw_loaded", "xr_loaded0", "xr_loaded1", "z_done", "z_squared", "z_mean", "z_rstd",
            "z_weighted", "row_left_done", "row_right_done", "row_stored0", "row_stored1", "vec_step", "act_step",
        ]
        S = {n: names.enter_context(nc.semaphore(n)) for n in sem_names}

        here = [16512]

        def at(name, shape, dtype, offset=None):
            size = 4 if dtype != U8 else 1
            for n in shape[1:]:
                size *= n
            if offset is None:
                offset = here[0]
                here[0] += (size + 31) // 32 * 32
            return nc.alloc_sbuf_tensor_at(name, shape, dtype, offset=offset), offset

        h_hi, _ = at("h_hi", [P, NK, L], F32R)
        h_lo, _ = at("h_lo", [P, NK, L], F32R)
        a_hi, a_hi_at = at("a_hi", [P, NK, SEQ], F32R)
        a_lo, a_lo_at = at("a_lo", [P, NK, SEQ], F32R)
        raw, _ = at("raw", [P, 2, D], F32)
        w_hi, _ = at("w_hi", [P, 2, D], F32R)
        w_lo, _ = at("w_lo", [P, 2, D], F32R)
        bias, _ = at("bias", [P, 8, 8], F32)
        cur, _ = at("cur", [P, 3, 8], F32)
        lb, _ = at("lb", [P, HEADS], F32)
        one_minus_lb, _ = at("one_minus_lb", [P, HEADS], F32)
        hgw, _ = at("hgw", [P, HEADS], F32)
        psc, _ = at("psc", [P, NK], F32)
        logits, _ = at("logits", [P, 2, HEADS], F32)
        lexp, _ = at("lexp", [P, 2, HEADS], F32)
        lmax, _ = at("lmax", [P, HEADS], F32)
        x_ss, _ = at("x_ss", [P, 16], F32)
        x_ms, _ = at("x_ms", [P, 16], F32)
        x_rs, _ = at("x_rs", [P, 16], F32)
        o_ss, _ = at("o_ss", [P, CHUNKS], F32)
        o_ms, _ = at("o_ms", [P, CHUNKS], F32)
        o_rs, _ = at("o_rs", [P, CHUNKS], F32)
        minus_half, _ = at("minus_half", [P, 16], F32)
        ident, _ = at("ident", [P, P], F32)
        top = here[0]

        fg, _ = at("fg", [P, L], F32)
        sn, _ = at("sn", [P, L], F32)
        qx, _ = at("qx", [P, 2, SEQ], F32)
        qt, qr = qx[:, 0, :], qx[:, 1, :]
        vt, _ = at("vt", [P, L], F32)
        gt, _ = at("gt", [P, SEQ], F32)
        gs, _ = at("gs", [P, HALF], F32)
        kt, _ = at("kt", [P, L], F32)
        tree, _ = at("tree", [P, L], F32)
        vv, _ = at("vv", [P, SEQ], F32)
        vm, _ = at("vm", [META, P], F32)
        km, _ = at("km", [META, P], F32)
        st, st_at = at("st", [P, SEQ], F32)
        on, _ = at("on", [P, SEQ], F32, st_at)
        prod, prod_at = at("prod", [P, HALF], F32)
        assert prod_at == st_at + 4 * SEQ
        qq, _ = at("qq", [P, CHUNKS, 3 * 64], F32, st_at)
        mask1, _ = at("mask1", [P, MASKS, 64], F32, prod_at)
        mask, _ = at("mask", [P, MASKS, HALF], U8)
        gm, _ = at("gm", [P, 2, HALF], F32)
        assert here[0] <= 229368, here[0]
        last = 4 * (NK - 1) * SEQ
        att, _ = at("att", [P, SEQ], F32, a_hi_at + last)
        ek, _ = at("ek", [P, SEQ], F32, a_lo_at + last)
        xin, _ = at("xin", [P, 3, D], F32, a_hi_at)
        nw, _ = at("nw", [P, D], F32, a_hi_at + 12288)
        hrow, _ = at("hrow", [P, 2, D], F32, a_hi_at + 16384)
        xsq, _ = at("xsq", [P, D], F32, a_hi_at + 24576)

        here[0] = top
        sm, _ = at("sm", [P, 2, HALF], F32)
        yb, _ = at("yb", [P, 2, HALF], F32)
        part, _ = at("part", [P, 2, HALF], F32)
        here[0] = top
        uu, _ = at("uu", [P, 2, L], F32)
        pool_a, _ = at("pool_a", [P, L], F32)
        pool_b, _ = at("pool_b", [P, L], F32)
        p_hi, _ = at("p_hi", [P, 2, SEQ], F32R)
        p_lo, _ = at("p_lo", [P, 2, SEQ], F32R)
        pg, _ = at("pg", [P, 2, SEQ], F32)
        pgs, _ = at("pgs", [P, HALF], F32)
        mx, _ = at("mx", [P, 2, HALF], F32)
        pw, _ = at("pw", [P, 512], F32)
        pw_hi, _ = at("pw_hi", [P, 512], F32R)
        pw_lo, _ = at("pw_lo", [P, 512], F32R)
        assert here[0] <= 229368, here[0]
        here[0] = top
        yp, yp_at = at("yp", [P, 2, HALF], F32)
        sp_in, _ = at("sp_in", [P, 2, HALF], F32)
        pt_in, _ = at("pt_in", [P, 2, HALF], F32)
        mg, _ = at("mg", [P, 2, HALF], F32)
        wo0_hi, _ = at("wo0_hi", [P, NK, HALF], F32R)
        wo0_lo, _ = at("wo0_lo", [P, NK, HALF], F32R)
        assert here[0] <= 229368, here[0]
        zz, _ = at("zz", [P, CHUNKS, HALF], F32, a_hi_at + 16384)
        z1, _ = at("z1", [P, 2, HALF], F32, a_lo_at + 16384)
        xr, _ = at("xr", [P, 2, HALF], F32, a_lo_at + 20480)
        fnw, _ = at("fnw", [P, D], F32, a_lo_at + 28672)
        row, _ = at("row", [P, 2, D], F32, yp_at)
        z_ss, _ = at("z_ss", [P, 2, CHUNKS], F32, yp_at + 8192)
        z_ms, _ = at("z_ms", [P, CHUNKS], F32, yp_at + 8320)
        z_rs, _ = at("z_rs", [P, CHUNKS], F32, yp_at + 8352)
        zsq, _ = at("zsq", [P, HALF], F32, yp_at + 8448)
        wo1_hi = a_hi[:, :, :].rearrange("p k t -> p (k t)")[:, 0:NK * HALF].rearrange("p (k n) -> p k n", k=NK)
        wo1_lo = a_lo[:, :, :].rearrange("p k t -> p (k t)")[:, 0:NK * HALF].rearrange("p (k n) -> p k n", k=NK)

        acc = [names.enter_context(nc.psum_tensor(f"acc{n}", [P, HALF], F32)) for n in range(4)]
        levels = names.enter_context(nc.psum_tensor("levels", [P, 2, HALF], F32))
        lev, small = levels[:, 0, :], levels[:, 1, :]
        miscs = names.enter_context(nc.psum_tensor("miscs", [P, 2, HALF], F32))
        misc = (miscs[:, 0, :], miscs[:, 1, :])
        VM, KM, KVM = slice(128, 256), slice(256, 384), slice(384, 512)
        h_banks = ((misc[0], misc[1]), (lev, small))

        smp_dram = nc.dram_tensor("smp_spill", [NK, 2, P, HALF], F32, kind="Internal").ap()
        part_dram = nc.dram_tensor("part_spill", [NK, 2, P, HALF], F32, kind="Internal").ap()

        raw_loaded = (S["raw_loaded0"], S["raw_loaded1"])
        x_loaded = (S["x_loaded0"], S["x_loaded1"], S["x_loaded2"])
        smp_stored = (S["smp_stored0"], S["smp_stored1"])
        part_stored = (S["part_stored0"], S["part_stored1"])
        spill_loaded = (S["spill_loaded0"], S["spill_loaded1"])
        xr_loaded = (S["xr_loaded0"], S["xr_loaded1"])
        row_stored = (S["row_stored0"], S["row_stored1"])

        def tile_of(i):
            return (META, 0) if i == 0 else (P, META + (i - 1) * P)

        def level_view(t, m, h):
            return t.rearrange("p (b h j) -> p b h j", h=2, j=1 << m)[:, :, h, :]

        def tree_at(m):
            if m == 0:
                return fg[:, :], META
            lo = sum(L >> n for n in range(1, min(m, 5))) + sum(SEQ >> n for n in range(5, m))
            with_meta = m <= 4
            n = (L if with_meta else SEQ) >> m
            return tree[:, lo:lo + n], (META >> m) if with_meta else 0

        block = names.enter_context(nc.Block())

        @block.sync
        def _(sp):
            sp.dma_start(xin[0:META, 0, :], meta[:, :]).then_inc(x_loaded[0], 16)
            sp.dma_start(xin[:, 1, :], x[0:P, :]).then_inc(x_loaded[1], 16)
            sp.dma_start(xin[:, 2, :], x[P:2 * P, :]).then_inc(x_loaded[2], 16)
            for b in range(2):
                sp.dma_start(raw[:, b, :], wstream[b]).then_inc(raw_loaded[b], 16)
            for i in range(3, CHUNKS + 1):
                sp.wait_ge(S["h_row"], i - 2)
                sp.dma_start(xin[:, i % 3, :], x[(i - 1) * P:i * P, :]).then_inc(x_loaded[i % 3], 16)
            with sp.Fori(1, BLKS // 2) as i:
                for s in range(2):
                    sp.wait_ge(S["w_lo_ready"], i * 2 + (s - 1))
                    sp.dma_start(raw[:, s, :], wstream[i * 2 + s]).then_inc(raw_loaded[s], 16)
            for t in range(CHUNKS):
                sp.wait_ge(S["row_left_done"], t + 1)
                sp.wait_ge(S["row_right_done"], t + 1)
                sp.dma_start(out[t * P:(t + 1) * P, :], row[:, t % 2, :]).then_inc(row_stored[t % 2], 16)
            for s in range(2):
                sp.wait_ge(row_stored[s], 16 * (CHUNKS // 2))

        @block.gpsimd
        def _(pool):
            steps = Steps(pool, S["pool_step"])
            steps.mark(pool.memset(ident[:, :], 0.0))
            steps.mark(pool.memset(minus_half[:, :], -0.5))
            steps.settle()
            pool.affine_select(out=ident[:, :], in_=ident[:, :], compare_op=ALU.not_equal, fill=1.0, base=0,
                               pattern=[[-1, P]], channel_multiplier=1).then_inc(S["consts_made"], 1)

            params = [(bias[:, :, :], b_in[:, :, :]), (hgw[:, :], hg_norm_w[:, :]),
                      (psc[:, :], pool_scale[:, :])]
            for dst, src in params:
                pool.dma_start(dst, src).then_inc(S["params_loaded"], 16)

            for i in range(CHUNKS + 1):
                rows = tile_of(i)[0]
                pool.wait_ge(S["x_mean"], i + 1)
                pool.tensor_tensor(x_rs[0:rows, i:i + 1], x_ms[0:rows, i:i + 1], minus_half[0:rows, 0:1],
                                   ALU.pow).then_inc(S["x_rstd"], 1)

            steps.mark(pool.memset(mask1[:, :, :], 1.0))

            def keep(mask, base, channel, pattern):
                steps.mark(pool.affine_select(out=mask, in_=mask, compare_op=ALU.is_ge, fill=0.0, base=base,
                                              pattern=pattern, channel_multiplier=channel))

            level0 = mask1[:, 0:2, :].rearrange("p a (b j) -> p (a b) j", j=2)
            odd = mask1[:, 3, :]
            halves = [(m, mask1[:, n, :].rearrange("p (b j) -> p b j", j=1 << m), lo, hi)
                      for m, n, lo, hi in ((1, 2, 0, 1), (2, 4, 0, 3), (3, 5, 4, 7), (3, 6, 0, 3), (4, 7, 0, 15))]
            steps.settle()
            keep(level0, 0, 1, [[-2, 64], [0, 2]])
            keep(odd, -1, 1, [[-2, 64]])
            for m, view, lo, _ in halves:
                keep(view, -lo, 1, [[-(2 << m), 64 >> m], [0, 1 << m]])
            steps.settle()
            keep(level0, 0, -1, [[2, 64], [0, 2]])
            keep(odd, 1, -1, [[2, 64]])
            for m, view, _, hi in halves:
                ins = pool.affine_select(out=view, in_=view, compare_op=ALU.is_ge, fill=0.0, base=hi,
                                         pattern=[[2 << m, 64 >> m], [0, 1 << m]], channel_multiplier=-1)
            ins.then_inc(S["masks_made"], 1)

            def o_rstd(r):
                pool.wait_ge(S["o_mean"], r + 1)
                pool.tensor_tensor(o_rs[:, :], o_ms[:, :], minus_half[:, 0:CHUNKS], ALU.pow).then_inc(S["o_rstd"], 1)

            with pool.Fori(0, HEADS - 1) as r:
                o_rstd(r)

            def store_smp(n, u):
                for h in range(2):
                    pool.wait_ge(S["acc_read"], u + h + 1)
                    pool.dma_start(smp_dram[n, h], gm[:, h, :]).then_inc(smp_stored[h], 16)

            for n in range(4):
                store_smp(n, HEADS * 10 + 2 * n)
            o_rstd(HEADS - 1)
            for n in range(4, NK):
                store_smp(n, U_TAIL + 2 * (n - 4))
            with pool.Fori(0, NK) as n:
                for h in range(2):
                    pool.wait_ge(S["part_made"], n * 2 + (h + 1))
                    pool.dma_start(part_dram[n, h], part[:, h, :]).then_inc(part_stored[h], 16)
            for h in range(2):
                pool.wait_ge(part_stored[h], 16 * NK)
                pool.wait_ge(smp_stored[h], 16 * NK)

            pool.dma_start(pw[:, :], pool_w[0]).then_inc(S["pw_loaded"], 16)
            with pool.Fori(1, 4) as g:
                pool.wait_ge(S["pw_lo_done"], g)
                pool.dma_start(pw[:, :], pool_w[g]).then_inc(S["pw_loaded"], 16)
            pool.wait_ge(S["c_done"], 16)

            def load_spills(n, h):
                pool.dma_start(sp_in[:, h, :], smp_dram[n, h]).then_inc(spill_loaded[h], 16)
                pool.dma_start(pt_in[:, h, :], part_dram[n, h]).then_inc(spill_loaded[h], 16)

            for h in range(2):
                load_spills(0, h)
            with pool.Fori(1, NK) as n:
                for h in range(2):
                    pool.wait_ge(S["merged_done"], n * 2 + (h - 1))
                    load_spills(n, h)
            pool.wait_ge(S["acc_done"], U_OUT)
            pool.dma_start(fnw[:, :], final_norm_w[0:1, :].to_broadcast([P, D])).then_inc(S["fnw_loaded"], 16)

            def residual(v):
                n, t = divmod(v, CHUNKS)
                after(pool, S["z_done"], v - 1)
                pool.dma_start(xr[:, v % 2, :], x[t * P:(t + 1) * P, n * HALF:(n + 1) * HALF]) \
                    .then_inc(xr_loaded[v % 2], 16)

            def z_rstd(t):
                pool.wait_ge(S["z_mean"], t + 1)
                pool.tensor_tensor(z_rs[:, t:t + 1], z_ms[:, t:t + 1], minus_half[:, 0:1], ALU.pow) \
                    .then_inc(S["z_rstd"], 1)

            for v in range(CHUNKS):
                residual(v)
            for v in range(CHUNKS, 2 * CHUNKS):
                residual(v)
                if v > CHUNKS:
                    z_rstd(v - CHUNKS - 1)
            z_rstd(CHUNKS - 1)

        @block.scalar
        def _(act):
            steps = Steps(act, S["act_step"])
            act.dma_start(nw[:, :], norm_w[0:1, :].to_broadcast([P, D])).then_inc(S["norm_row_loaded"], 16)
            act.dma_start(logits[:, :, :], lb_logits[:, :, :]).then_inc(S["logits_loaded"], 16)

            def split_hi(b, slot, free, dst=None, left=None):
                if left is not None:
                    act.wait_ge(S["acc_read"], left)
                act.wait_ge(raw_loaded[slot], b * 8 + (16 - 8 * slot))
                after(act, S["acc_done"], free)
                src = raw[:, slot, :] if dst is None else raw[:, slot, :].rearrange("p (k n) -> p k n", k=2)
                act.activation(w_hi[:, slot, :] if dst is None else dst, src, ACT.Copy).then_inc(S["w_hi_ready"], 1)

            def square_x(i):
                rows = tile_of(i)[0]
                act.wait_ge(x_loaded[i % 3], 16 * (i // 3 + 1))
                if i:
                    act.wait_ge(S["x_squared"], i)
                act.activation(xsq[0:rows, :], xin[0:rows, i % 3, :], ACT.Square,
                               accum_out=x_ss[0:rows, i:i + 1]).then_inc(S["x_squared"], 1)

            def h_high(i):
                rows, col = tile_of(i)
                act.wait_ge(S["h_tr"], i + 1)
                for q in range(2):
                    src = h_banks[i % 2][q][:, :].rearrange("p (k t) -> p k t", k=4)[:, :, 0:rows]
                    ins = act.activation(h_hi[:, 4 * q:4 * q + 4, col:col + rows], src, ACT.Copy)
                ins.then_inc(S["h_hi_done"], 1)

            square_x(0)
            square_x(1)
            square_x(2)
            split_hi(0, 0, 0)
            h_high(0)
            h_high(1)
            h_high(2)
            square_x(3)
            square_x(4)
            split_hi(1, 1, 0)
            act.wait_ge(S["lb_shifted"], 1)
            act.activation(lexp[:, :, :], lexp[:, :, :], ACT.Exp).then_inc(S["lb_exp"], 1)
            square_x(5)

            act.wait_ge(S["params_loaded"], 48)

            def biases(n, before=None, negate=False):
                def copied(row, m, scale):
                    one = ds(m, 1) if not isinstance(m, int) else slice(m, m + 1)
                    steps.mark(act.activation(cur[:, row:row + 1, :], bias[:, one, :], ACT.Copy, scale=scale))

                copied(0, n, 1.0)
                if negate:
                    copied(1, n, -1.0)
                if before is not None:
                    copied(2, before, 1.0)
                steps.settle()

            def leave(u, bank, dst, n, func, part=None, row=0):
                act.wait_ge(S["acc_done"], u + 1)
                b = 0.0 if part is None else cur[:, row, part:part + 1]
                return act.activation(dst, acc[bank][:, 0:n], func, bias=b)

            def leave_f(u, cols, bank):
                c0, n = cols
                leave(u, bank, fg[:, c0:c0 + n], n, ACT.Sigmoid, F)
                act.activation(sn[:, c0:c0 + n], acc[bank][:, 0:n], ACT.Sigmoid, bias=cur[:, 1, F:F + 1],
                               scale=-1.0).then_inc(S["acc_read"], 1)

            def leave_v(u, cols, bank):
                c0, n = cols
                leave(u, bank, vt[:, c0:c0 + n], n, ACT.Identity, V).then_inc(S["acc_read"], 1)

            def leave_q(u, k, bank):
                leave(u, bank, qr[:, k * HALF:(k + 1) * HALF], HALF, ACT.Identity, Q) \
                    .then_inc(S["acc_read"], 1)

            def leave_g(r, u, k):
                after(act, S["a_done"], r * 2)
                after(act, S["gate_done"], r * 2 + k)
                leave(u + 8 + k, BANKS10[8 + k], gt[:, k * HALF:(k + 1) * HALF], HALF, ACT.Identity, G, 2)
                act.activation(gs[:, :], acc[BANKS10[8 + k]][:, :], ACT.Sigmoid, bias=cur[:, 2, G:G + 1]) \
                    .then_inc(S["acc_read"], 1)

            def leave_gm(n, u, banks):
                act.wait_ge(S["acc_read"], u)
                biases(n, HEADS - 1)
                for h in range(2):
                    after(act, smp_stored[h], 16 * n)
                    leave(u + h, banks[h], gm[:, h, :], HALF, ACT.Sigmoid, MP) \
                        .then_inc(S["acc_read"], 1)

            def copy_v(r):
                act.wait_ge(S["v_tr"], r + 1)
                for q in range(2):
                    act.activation(vv[:, q * HALF:(q + 1) * HALF], misc[q][:, :], ACT.Copy)
                act.activation(vm[:, :], small[0:META, VM], ACT.Copy).then_inc(S["v_copied"], 1)

            def copy_k(r):
                act.wait_ge(S["k_tr"], r + 1)
                for q in range(2):
                    act.activation(ek[:, q * HALF:(q + 1) * HALF], misc[q][:, :], ACT.Copy)
                act.activation(km[:, :], small[0:META, KM], ACT.Copy).then_inc(S["k_copied"], 1)

            def square_o(r):
                act.wait_ge(S["o_mm"], r + 1)
                for q in range(2):
                    ins = act.activation(ek[:, q * HALF:(q + 1) * HALF], misc[q][:, :], ACT.Square)
                ins.then_inc(S["o_squared"], 1)

            biases(0, negate=True)
            for k, cols in enumerate(FIRST):
                if k < 3:
                    h_high(2 * k + 3)
                    h_high(2 * k + 4)
                if k < 2:
                    square_x(2 * k + 6)
                if k == 3:
                    split_hi(2, 0, 7)
                leave_f(2 * k, cols, BANKS10[2 * k])
                if k == 0:
                    square_x(7)
                leave_v(2 * k + 1, cols, BANKS10[2 * k + 1])
            act.wait_ge(S["masks_made"], 1)
            src = mask1[:, :, :].rearrange("p m (o t) -> p m o t", o=1).to_broadcast([P, MASKS, CHUNKS, 64])
            act.activation(mask[:, :, :].rearrange("p m (c t) -> p m c t", c=CHUNKS), src, ACT.Copy) \
                .then_inc(S["masks_spread"], 1)
            split_hi(3, 1, 8)
            for k in range(2):
                leave_q(8 + k, k, BANKS10[8 + k])

            def head_body(j):
                r, u, b = j - 1, j * 10, first_block(j)
                copy_v(r)
                split_hi(b + 1, 0, u, left=u)
                biases(j, r, negate=True)
                act.wait_ge(S["level_done"], r * STEPS + 1)
                for k in range(3):
                    leave_f(u + k, WITH_META[k], BANKS10[k])
                split_hi(b + 2, 1, u + 3)
                for k in range(3):
                    leave_v(u + 3 + k, WITH_META[k], BANKS10[3 + k])
                split_hi(b + 3, 0, u + 6)
                act.wait_ge(S["level_done"], r * STEPS + 2)
                leave_q(u + 6, 0, BANKS10[6])
                copy_k(r)
                leave_q(u + 7, 1, BANKS10[7])
                split_hi(b + 4, 1, u + 8)
                leave_g(r, u, 0)
                square_o(r)
                leave_g(r, u, 1)

            head_body(1)
            with act.Fori(2, HEADS) as j:
                steps.enter(j, 2, 3)
                head_body(j)
            steps.leave(3, HEADS - 2)
            r, u, b = HEADS - 1, HEADS * 10, first_block(HEADS)
            copy_v(r)
            for n in range(4):
                split_hi(b + n + 1, (n + b + 1) % 2, u + 2 * n)
                if n < 3:
                    leave_gm(n, u + 2 * n, BANKS10[2 * n:])
            copy_k(r)
            leave_gm(3, u + 6, BANKS10[6:])
            split_hi(b + 5, 0, u + 8)
            leave_g(r, u, 0)
            square_o(r)
            leave_g(r, u, 1)
            for n in range(4):
                split_hi(BLK_TAIL + n + 1, (n + 1) % 2, U_TAIL + 2 * n)
                leave_gm(4 + n, U_TAIL + 2 * n, BANKS8[2 * n:])

            act.wait_ge(S["a_done"], 2 * HEADS)

            def mix_body(n, free):
                b, u = n * 2 + BLK_MIX, n * 4 + U_MIX
                split_hi(b + 1, 1, u, left=u)
                biases(n)
                for h in range(2):
                    after(act, S["part_made"], free + h)
                    leave(u + h, h, sm[:, h, :], HALF, ACT.Sigmoid, MH).then_inc(S["acc_read"], 1)
                split_hi(b + 2, 0, u + 2)
                for h in range(2):
                    leave(u + 2 + h, 2 + h, yb[:, h, :], HALF, ACT.Copy).then_inc(S["acc_read"], 1)

            mix_body(0, -1)
            with act.Fori(1, NK) as n:
                steps.enter(n, 1, 1)
                mix_body(n, n * 2 - 1)
            steps.leave(1, NK - 1)

            for h in range(2):
                act.wait_ge(part_stored[h], 16 * NK)
                act.wait_ge(smp_stored[h], 16 * NK)

            def pool_body(g):
                b, u = g * 4 + BLK_POOL, g * 14 + U_POOL
                split_hi(b + 1, 1, u, left=u)
                biases(g * 2, g * 2 + 1)
                after(act, S["pooled_done"], g * 2)
                for k in range(3):
                    c0, n = WITH_META[k]
                    leave(u + k, BANKS14[k], uu[:, 0, c0:c0 + n], n, ACT.Identity, U) \
                        .then_inc(S["acc_read"], 1)
                split_hi(b + 2, 0, u + 3)
                for k in range(3):
                    c0, n = WITH_META[k]
                    leave(u + 3 + k, BANKS14[3 + k], uu[:, 1, c0:c0 + n], n, ACT.Identity, U, 2) \
                        .then_inc(S["acc_read"], 1)
                split_hi(b + 3, 1, u + 6)
                act.wait_ge(S["pw_loaded"], g * 16 + 16)
                act.activation(pw_hi[:, :], pw[:, :], ACT.Copy).then_inc(S["pw_hi_done"], 1)
                after(act, S["c_done"], g * 4)
                for k in range(4):
                    if k == 2:
                        split_hi(b + 4, 0, u + 8)
                    row = 2 * (k // 2)
                    after(act, S["pgate_done"], g * 4 + k)
                    leave(u + 6 + k, BANKS14[6 + k], pg[:, k // 2, (k % 2) * HALF:(k % 2 + 1) * HALF], HALF,
                          ACT.Identity, PG, row)
                    act.activation(pgs[:, :], acc[BANKS14[6 + k]][:, :], ACT.Sigmoid, bias=cur[:, row, PG:PG + 1]) \
                        .then_inc(S["acc_read"], 1)
                for k in range(4):
                    after(act, S["c_done"], g * 4 + (k - 1))
                    leave(u + 10 + k, BANKS14[10 + k], mx[:, k % 2, :], HALF, ACT.Copy).then_inc(S["acc_read"], 1)

            pool_body(0)
            with act.Fori(1, 4) as g:
                steps.enter(g, 1, 2)
                pool_body(g)
            steps.leave(2, 3)

            act.wait_ge(S["c_done"], 16)

            def down_block(n, bank, split):
                split()
                for h in range(2):
                    after(act, S["merged_done"], n * 2 + (h - 1))
                    leave(n * 2 + (U_DOWN + h), bank + h, yp[:, h, :], HALF, ACT.Copy).then_inc(S["acc_read"], 1)

            down_block(0, 0, lambda: split_hi(BLK_DOWN + 1, 1, U_DOWN))
            down_block(1, 2, lambda: split_hi(BLK_DOWN + 2, 0, U_DOWN + 2))
            with act.Fori(1, NK // 2 - 1) as i:
                for s in range(2):
                    down_block(i * 2 + s, 2 * s,
                               lambda: split_hi(i * 2 + (BLK_DOWN + s + 1), 1 - s, i * 4 + (U_DOWN + 2 * s)))

            def split_out(q):
                split_hi(BLK_OUT + q, q % 2, 0, wo0_hi[:, 2 * q:2 * q + 2, :])

            def split_last():
                split_hi(BLK_OUT - 1, 1, U_OUT - 4)
                split_out(0)
                split_out(1)

            def split_rest():
                split_out(2)
                split_out(3)

            down_block(NK - 2, 0, split_last)
            down_block(NK - 1, 2, split_rest)

            def square_z(v):
                n, t = divmod(v, CHUNKS)
                act.wait_ge(S["z_done"], v + 1)
                if v:
                    act.wait_ge(S["z_squared"], v)
                src = zz[:, t, :] if n == 0 else z1[:, t % 2, :]
                act.activation(zsq[:, :], src, ACT.Square, accum_out=z_ss[:, n, t:t + 1]).then_inc(S["z_squared"], 1)

            for q in range(4):
                split_hi(BLK_OUT + 4 + q, q % 2, U_OUT, wo1_hi[:, 2 * q:2 * q + 2, :])
            act.wait_ge(S["merged_done"], 2 * NK)
            for v in range(2 * CHUNKS):
                square_z(v)
                if v >= CHUNKS:
                    t = v - CHUNKS
                    act.wait_ge(S["z_weighted"], t + 1)
                    act.wait_ge(S["z_rstd"], t + 1)
                    after(act, row_stored[t % 2], 16 * (t // 2))
                    act.activation(row[:, t % 2, 0:HALF], zz[:, t, :], ACT.Copy, scale=z_rs[:, t:t + 1]) \
                        .then_inc(S["row_left_done"], 1)

        @block.tensor
        def _(pe):
            def three(out_ap, lhs, rhs, first, final):
                pairs = ((lhs[0], rhs[0]), (lhs[0], rhs[1]), (lhs[1], rhs[0]))
                for n, (a, b) in enumerate(pairs):
                    ins = pe.matmul(out_ap, a, b, start=first and n == 0, stop=final and n == 2)
                return ins

            def half_unit(u, bank, slot, rhs, cols, part, late=None):
                c0, n = cols
                if part == 0:
                    after(pe, S["acc_read"], u - 2)
                for k in range(4 * part, 4 * part + 4):
                    if late is not None and k == late[0]:
                        pe.wait_ge(late[1], late[2])
                    w = slice(k * P, (k + 1) * P)
                    ins = three(acc[bank][:, 0:n], (w_hi[:, slot, w], w_lo[:, slot, w]),
                                (rhs[0][:, k, c0:c0 + n], rhs[1][:, k, c0:c0 + n]), k == 0, k == NK - 1)
                if part == 1:
                    ins.then_inc(S["acc_done"], 1)

            def unit(u, bank, slot, rhs, cols):
                for part in range(2):
                    half_unit(u, bank, slot, rhs, cols, part)

            def weights(b):
                pe.wait_ge(S["w_lo_ready"], b + 1)

            def h_transposes(i):
                rows = tile_of(i)[0]
                pe.wait_ge(S["h_row"], i + 1)
                after(pe, S["h_lo_done"], i - 1)
                for k in range(NK):
                    o = (k % 4) * P
                    ins = pe.transpose(h_banks[i % 2][k // 4][:, o:o + rows], hrow[0:rows, i % 2, k * P:(k + 1) * P],
                                       ident[0:rows, 0:rows])
                ins.then_inc(S["h_tr"], 1)

            def v_transposes(r):
                pe.wait_ge(S["acc_read"], v_read(r))
                after(pe, S["o_normed"], r)
                for c in range(CHUNKS):
                    pe.transpose(misc[c // 4][:, (c % 4) * P:(c % 4 + 1) * P],
                                 vt[:, META + c * P:META + (c + 1) * P], ident[:, :])
                pe.transpose(small[0:META, VM], vt[:, 0:META], ident[:, :]).then_inc(S["v_tr"], 1)

            def step(r, i):
                m = STEP_LEVEL[i]
                if m:
                    pe.wait_ge(S["level_done"], r * STEPS + i)
                else:
                    pe.wait_ge(S["prepared"], r + 1)
                    pe.wait_ge(S["v_copied"], r + 1)
                if m == 2:
                    after(pe, S["a_done"], r * 2)
                for c in range(CHUNKS):
                    s, ks = slice(c * P, (c + 1) * P), slice(META + c * P, META + (c + 1) * P)
                    if m < 2:
                        q = ek[:, s] if m == 0 else \
                            qx[:, :, s].rearrange("p a (b h j) -> p a b h j", h=2, j=2)[:, :, :, 1, :]
                        ins = pe.matmul((lev, small)[c // 4][:, (c % 4) * P:(c % 4 + 1) * P], kt[:, ks], q,
                                        start=True, stop=True)
                        continue
                    if m == 2:
                        bank = (lev, small, misc[0], misc[1])[c // 2]
                        ins = pe.matmul(bank[:, c % 2 * 192:(c % 2 + 1) * 192], kt[:, ks], qq[:, c, :],
                                        start=True, stop=True)
                        continue
                    halves = 1 if m == LEVELS - 1 else 2
                    rows, n = P // halves - (1 << m), 64 // halves
                    q = level_view(qt[:, s], m, 1).rearrange("p (g b) j -> p g b j", g=halves)
                    for h in range(halves):
                        s0, o = h * 64, c * 64 + h * n
                        ins = pe.matmul(lev[s0:s0 + rows, o:o + n], kt[:, META + c * P + s0:META + c * P + s0 + rows],
                                        q[:, h], start=True, stop=True)
                ins.then_inc(S["level_mm"], 1)

            def k_transposes(r):
                pe.wait_ge(S["level_done"], (r + 1) * STEPS)
                after(pe, S["a_done"], r * 2)
                for c in range(CHUNKS):
                    pe.transpose(misc[c // 4][:, (c % 4) * P:(c % 4 + 1) * P],
                                 kt[:, META + c * P:META + (c + 1) * P], ident[:, :])
                pe.transpose(small[0:META, KM], kt[:, 0:META], ident[:, :]).then_inc(S["k_tr"], 1)

            def k_times_v(r):
                pe.wait_ge(S["k_copied"], r + 1)
                pe.matmul(small[:, KVM], km[:, :], vm[:, :], start=True, stop=True)
                for c in range(CHUNKS - 1):
                    s = slice(c * P, (c + 1) * P)
                    ins = pe.matmul(misc[c // 4][:, (c % 4) * P:(c % 4 + 1) * P], ek[:, s], vv[:, s],
                                    start=True, stop=True)
                ins.then_inc(S["kv_mm"], 1)

            def outputs(r):
                pe.wait_ge(S["state_done"], r + 1)
                for c in range(CHUNKS):
                    s = slice(c * P, (c + 1) * P)
                    dst = misc[c // 4][:, (c % 4) * P:(c % 4 + 1) * P]
                    pe.matmul(dst, qt[:, s], st[:, s], start=True, stop=False)
                    ins = pe.matmul(dst, att[:, s], vv[:, s], start=False, stop=True)
                ins.then_inc(S["o_mm"], 1)

            def o_transposes(r, v_next):
                pe.wait_ge(S["o_normed"], r + 1)
                if v_next:
                    pe.wait_ge(S["v_copied"], r + 2)
                for c in range(CHUNKS):
                    ins = pe.transpose(misc[c // 4][:, (c % 4) * P:(c % 4 + 1) * P], on[:, c * P:(c + 1) * P],
                                       ident[:, :])
                ins.then_inc(S["o_tr"], 1)

            def stage(pos, r, o_before):
                if pos == 1:
                    v_transposes(r)
                elif pos in STEP_AT:
                    step(r, STEP_AT.index(pos))
                elif pos == 3 and o_before:
                    o_transposes(r - 1, True)
                elif pos == 15:
                    k_transposes(r)
                elif pos == 16:
                    k_times_v(r)
                elif pos == 18:
                    outputs(r)

            hs, aa = (h_hi, h_lo), (a_hi, a_lo)
            head_blocks = ((0, WITH_META), (3, WITH_META), (6, NO_META), (8, NO_META))
            pe.wait_ge(S["consts_made"], 1)
            def keep_warm(n):
                for _ in range(n):
                    pe.matmul(acc[3][:, 0:P], ident[:, :], ident[:, :], start=True, stop=True)

            for i in range(3):
                keep_warm(WARM_UP[i])
                h_transposes(i)
            keep_warm(WARM_UP[3])
            for k, cols in enumerate(FIRST):
                pe.wait_ge(S["h_lo_done"], 2 * k + 3)
                for blk in range(2):
                    if k == 0:
                        weights(blk)
                    u = 2 * k + blk
                    if (k, blk) in ((0, 1), (1, 0), (2, 1)):
                        h_transposes(u + 3)
                    half_unit(u, BANKS10[u], blk, hs, cols, 0)
                    if k < 3 and blk == 0:
                        h_transposes(u + (4 if k == 1 else 3))
                    half_unit(u, BANKS10[u], blk, hs, cols, 1)
            weights(2)
            for k, cols in enumerate(NO_META):
                unit(8 + k, BANKS10[8 + k], 0, hs, cols)

            def head_body(j, o_before):
                u, b = j * 10, first_block(j)
                for blk, (u0, cols) in enumerate(head_blocks):
                    for k, c in enumerate(cols):
                        for part in range(2):
                            stage(2 * (u0 + k) + part, j - 1, o_before)
                            if k == 0 and part == 0:
                                weights(b + blk)
                            half_unit(u + (u0 + k), BANKS10[u0 + k], (blk + 1) % 2, hs, c, part)

            head_body(1, False)
            with pe.Fori(2, HEADS) as j:
                head_body(j, True)
            u, b = HEADS * 10, first_block(HEADS)
            for k in range(10):
                for part in range(2):
                    stage(2 * k + part, HEADS - 1, True)
                    if k % 2 == 0 and part == 0:
                        weights(b + k // 2)
                    half_unit(u + k, BANKS10[k], (k // 2 + 1) % 2, hs, NO_META[k % 2], part)
            for k in range(8):
                if k % 2 == 0:
                    weights(BLK_TAIL + k // 2)
                unit(U_TAIL + k, BANKS8[k], (k // 2) % 2, hs, NO_META[k % 2])
                if k == 0:
                    o_transposes(HEADS - 1, False)

            pe.wait_ge(S["a_done"], 2 * HEADS)
            with pe.Fori(0, NK) as n:
                weights(n * 2 + BLK_MIX)
                for h in range(2):
                    unit(n * 4 + (U_MIX + h), h, 0, hs, NO_META[h])
                weights(n * 2 + (BLK_MIX + 1))
                for h in range(2):
                    unit(n * 4 + (U_MIX + 2 + h), 2 + h, 1, aa, (h * HALF, HALF))

            with pe.Fori(0, 4) as g:
                u, b = g * 14 + U_POOL, g * 4 + BLK_POOL
                for blk, (u0, cols) in enumerate(((0, WITH_META), (3, WITH_META), (6, NO_META), (8, NO_META))):
                    weights(b + blk)
                    for k, c in enumerate(cols):
                        unit(u + (u0 + k), BANKS14[u0 + k], blk % 2, hs, c)
                pe.wait_ge(S["pooled_done"], g * 2 + 2)
                pe.wait_ge(S["pw_lo_done"], g + 1)
                for k in range(4):
                    o, c0 = k // 2, (k % 2) * HALF
                    pe.wait_ge(S["acc_read"], u + (8 + k))
                    for i in range(2):
                        w = slice(i * 256 + o * P, i * 256 + (o + 1) * P)
                        ins = three(acc[BANKS14[10 + k]][:, :], (pw_hi[:, w], pw_lo[:, w]),
                                    (p_hi[:, i, c0:c0 + HALF], p_lo[:, i, c0:c0 + HALF]), i == 0, i == 1)
                    ins.then_inc(S["acc_done"], 1)

            pe.wait_ge(S["c_done"], 12)
            with pe.Fori(0, NK // 2) as i:
                for s in range(2):
                    weights(i * 2 + (BLK_DOWN + s))
                    for part in range(2):
                        for h in range(2):
                            half_unit(i * 4 + (U_DOWN + 2 * s + h), 2 * s + h, s, aa, (h * HALF, HALF), part,
                                      (6, S["c_done"], 16))

            pe.wait_ge(S["merged_done"], 2 * NK - 2)
            for n, wo in enumerate(((wo0_hi, wo0_lo), (wo1_hi, wo1_lo))):
                for t in range(CHUNKS):
                    v = n * CHUNKS + t
                    if v < 3:
                        pe.wait_ge(S["acc_read"], U_OUT + v - 2)
                    else:
                        pe.wait_ge(S["z_done"], v - 2)
                    s = slice(META + t * P, META + (t + 1) * P)
                    for k in range(NK):
                        if t == 0 and k % 2 == 0:
                            weights(BLK_OUT + 4 * n + k // 2)
                        if v in (0, 4) and k == NK - 1:
                            pe.wait_ge(S["merged_done"], 2 * NK - 1 + v // 4)
                        ins = three(acc[v % 4][:, :], (h_hi[:, k, s], h_lo[:, k, s]), (wo[0][:, k, :], wo[1][:, k, :]),
                                    k == 0, k == NK - 1)
                    ins.then_inc(S["acc_done"], 1)

        @block.vector
        def _(dve):
            steps = Steps(dve, S["vec_step"])
            steps.mark(dve.memset(att[:, :], 0.0))
            def x_mean(i):
                rows = tile_of(i)[0]
                dve.wait_ge(S["x_squared"], i + 1)
                dve.tensor_scalar(x_ms[0:rows, i:i + 1], x_ss[0:rows, i:i + 1], 1.0 / D, EPS, ALU.mult, ALU.add) \
                    .then_inc(S["x_mean"], 1)

            def h_row(i):
                rows = tile_of(i)[0]
                dve.wait_ge(S["x_rstd"], i + 1)
                after(dve, S["h_tr"], i - 1)
                dve.scalar_tensor_tensor(hrow[0:rows, i % 2, :], xin[0:rows, i % 3, :], x_rs[0:rows, i:i + 1],
                                         nw[0:rows, :], ALU.mult, ALU.mult).then_inc(S["h_row"], 1)

            def h_low(i):
                rows, col = tile_of(i)
                dve.wait_ge(S["h_hi_done"], i + 1)
                for q in range(2):
                    src = h_banks[i % 2][q][:, :].rearrange("p (k t) -> p k t", k=4)[:, :, 0:rows]
                    ks, ts = slice(4 * q, 4 * q + 4), slice(col, col + rows)
                    ins = dve.tensor_tensor(h_lo[:, ks, ts], src, h_hi[:, ks, ts].bitcast(F32), ALU.subtract)
                ins.then_inc(S["h_lo_done"], 1)

            def split_lo(b, slot, dst=None, hi=None):
                dve.wait_ge(S["w_hi_ready"], b + 1)
                src = raw[:, slot, :]
                if dst is None:
                    dst, hi = w_lo[:, slot, :], w_hi[:, slot, :]
                else:
                    src = src.rearrange("p (k n) -> p k n", k=2)
                dve.tensor_tensor(dst, src, hi.bitcast(F32), ALU.subtract).then_inc(S["w_lo_ready"], 1)

            x_mean(0)
            dve.wait_ge(S["norm_row_loaded"], 16)
            h_row(0)
            x_mean(1)
            h_row(1)
            x_mean(2)
            h_row(2)
            h_low(0)
            split_lo(0, 0)
            h_low(1)
            h_low(2)
            x_mean(3)
            dve.wait_ge(S["logits_loaded"], 16)
            steps.mark(dve.tensor_tensor(lmax[:, :], logits[:, 0, :], logits[:, 1, :], ALU.max))
            steps.settle()
            for n in range(2):
                ins = dve.tensor_tensor(lexp[:, n, :], logits[:, n, :], lmax[:, :], ALU.subtract)
            ins.then_inc(S["lb_shifted"], 1)
            h_row(3)
            x_mean(4)
            split_lo(1, 1)
            for i in range(4, CHUNKS + 1):
                if i != 7:
                    h_row(i)
                h_low(i - 1)
                if i == 7:
                    h_row(i)
                if i < CHUNKS:
                    x_mean(i + 1)
            h_low(CHUNKS)
            dve.wait_ge(S["params_loaded"], 48)

            dve.wait_ge(S["lb_exp"], 1)
            steps.mark(dve.tensor_tensor(lmax[:, :], lexp[:, 0, :], lexp[:, 1, :], ALU.add))
            steps.settle()
            steps.mark(dve.reciprocal(lmax[:, :], lmax[:, :]))
            steps.settle()
            steps.mark(dve.tensor_tensor(lb[:, :], lexp[:, 0, :], lmax[:, :], ALU.mult))
            steps.settle()
            steps.mark(dve.tensor_scalar(one_minus_lb[:, :], lb[:, :], -1.0, 1.0, ALU.mult, ALU.add))

            def prepare_gates(r, u):
                dve.wait_ge(S["acc_read"], u)
                one = ds(r, 1)
                steps.mark(dve.tensor_scalar(kt[:, :], sn[:, :], one_minus_lb[:, one], None, ALU.mult))
                steps.mark(dve.tensor_scalar(fg[:, :], fg[:, :], one_minus_lb[:, one], lb[:, one], ALU.mult, ALU.add))

            def prepare(r):
                dve.wait_ge(S["acc_read"], q_read(r))
                steps.settle()
                even, odd = level_view(ek[:, :], 0, 0), level_view(ek[:, :], 0, 1)
                steps.mark(dve.tensor_tensor(qt, qr, fg[:, META:L], ALU.mult))
                steps.mark(dve.tensor_copy(even, level_view(qr, 0, 0)))
                steps.settle()
                dve.tensor_copy(odd, level_view(qt, 0, 1))
                fours = qr.rearrange("p (b j) -> p b j", j=4)
                dve.tensor_copy(fours[:, :, 2:3], fours[:, :, 1:2]).then_inc(S["prepared"], 1)

            def entries(m, scale_k):
                if m != 1:
                    scale_k()
                if m < 2:
                    for q, bank in enumerate((lev, small)):
                        s = slice(q * HALF, (q + 1) * HALF)
                        a, p = att[:, s], bank[:, :]
                        if m == 0:
                            keep = mask[:, 0:2, 0:256].rearrange("p a (c t) -> p c a t", t=64)
                            steps.mark(dve.copy_predicated(a.rearrange("p (c a t) -> p c a t", a=2, t=64), keep,
                                                           p.rearrange("p (c a t) -> p c a t", a=2, t=64)))
                            continue
                        p = p.rearrange("p (c a t) -> p c a t", a=2, t=64)
                        keep = mask[:, 2:4, 0:256].rearrange("p a (c t) -> p a c t", t=64)
                        fours = a.rearrange("p (c b h j) -> p c b h j", b=32, h=2, j=2)[:, :, :, 1, :]
                        steps.mark(dve.copy_predicated(fours, keep[:, 0].rearrange("p c (b j) -> p c b j", j=2),
                                                       p[:, :, 0, :].rearrange("p c (b j) -> p c b j", j=2)))
                    if m == 1:
                        steps.settle()
                        scale_k()
                        for q, bank in enumerate((lev, small)):
                            p = bank[:, :].rearrange("p (c a t) -> p c a t", a=2, t=64)
                            odd = att[:, q * HALF:(q + 1) * HALF].rearrange("p (c t h) -> p c t h", t=64, h=2)
                            keep = mask[:, 3, 0:256].rearrange("p (c t) -> p c t", t=64)
                            steps.mark(dve.copy_predicated(odd[:, :, :, 1], keep, p[:, :, 1, :]))
                    return
                a, p = level_view(att[:, :], m, 1), lev[:, :].rearrange("p (b j) -> p b j", j=1 << m)
                if m < LEVELS - 2:
                    keep = mask[:, MASKS - 1, :].rearrange("p (b j) -> p b j", j=1 << m)
                    steps.mark(dve.copy_predicated(a, keep, p))
                    return
                for h in range(1 if m == LEVELS - 1 else 2):
                    rows = slice(h * (2 << m), h * (2 << m) + (1 << m))
                    if m == LEVELS - 2:
                        ah, ph = (v.rearrange("p (c g) j -> p c g j", g=2)[rows, :, h, :] for v in (a, p))
                    else:
                        ah, ph = a[rows], p[rows]
                    steps.mark(dve.tensor_copy(ah, ph))

            def level(r, m):
                now, x0 = tree_at(m)
                up, _ = tree_at(m + 1)
                pairs = now if m <= 3 else now[:, x0:]
                pairs = pairs.rearrange("p (b h) -> p b h", h=2)
                dve.wait_ge(S["level_mm"], r * STEPS + (STEP_LEVEL.index(m) + 1))
                steps.mark(dve.tensor_tensor(up, pairs[:, :, 0], pairs[:, :, 1], ALU.mult))
                j = 1 << m
                keys = kt[:, :] if m <= 3 else kt[:, META:L]
                nb = (L if m <= 3 else SEQ) >> (m + 1)
                ks = level_view(keys, m, 0)
                entries(m, lambda: dve.tensor_tensor(ks, ks, pairs[:, :, 1:2].to_broadcast([P, nb, j]), ALU.mult))
                queries = now[:, x0:].rearrange("p (b h) -> p b h", h=2)
                qs = level_view(qt, m, 1)
                ins = dve.tensor_tensor(qs, qs, queries[:, :, 0:1].to_broadcast([P, SEQ >> (m + 1), j]), ALU.mult)
                if m == 1:
                    steps.mark(ins)
                    ins = spread_queries()
                ins.then_inc(S["level_done"], 1)
                steps.settle()

            def quarter(n, j):
                return qq[:, :, n * 64:(n + 1) * 64].rearrange("p c (b j) -> p c b j", j=j)

            def spread_queries():
                f4, x4 = tree_at(2)
                halves = f4[:, x4:].rearrange("p (b h) -> p b h", h=2)
                quarters = f4[:, x4:].rearrange("p (c b h) -> p c b h", c=CHUNKS, h=4)
                qs = level_view(qt, 2, 1)
                steps.settle()
                steps.mark(dve.tensor_copy(quarter(0, 4), qs.rearrange("p (c b) j -> p c b j", c=CHUNKS)))
                steps.settle()
                steps.mark(dve.tensor_tensor(qs, qs, halves[:, :, 0:1].to_broadcast([P, SEQ // 8, 4]), ALU.mult))
                steps.settle()
                second = level_view(qt, 3, 1).rearrange("p (c b) j -> p c b j", c=CHUNKS)
                dve.tensor_copy(quarter(1, 8), second)
                between = quarters[:, :, :, 1:2].to_broadcast([P, CHUNKS, 8, 8])
                return dve.tensor_tensor(quarter(2, 8), second, between, ALU.mult)

            def levels_2_and_3(r):
                dve.wait_ge(S["level_mm"], r * STEPS + 3)
                fours, _ = tree_at(2)
                eights, x8 = tree_at(3)
                sixteens, _ = tree_at(4)
                fours = fours.rearrange("p (b h) -> p b h", h=2)
                pairs = eights.rearrange("p (b h) -> p b h", h=2)
                queries = eights[:, x8:].rearrange("p (b h) -> p b h", h=2)

                def part(n, m):
                    for b, bank in enumerate((lev, small, misc[0], misc[1])):
                        a = level_view(att[:, b * 2 * P:(b + 1) * 2 * P], m, 1).rearrange("p (c b) j -> p c b j", c=2)
                        keep = mask[:, 4 + n, 0:2 * 64].rearrange("p (c b j) -> p c b j", c=2, j=1 << m)
                        found = bank[:, 0:2 * 192].rearrange("p (c n t) -> p c n t", c=2, n=3)[:, :, n, :]
                        steps.mark(dve.copy_predicated(a, keep, found.rearrange("p c (b j) -> p c b j", j=1 << m)))

                steps.mark(dve.tensor_tensor(eights, fours[:, :, 0], fours[:, :, 1], ALU.mult))
                ks = level_view(kt[:, :], 2, 0)
                steps.mark(dve.tensor_tensor(ks, ks, fours[:, :, 1:2].to_broadcast([P, L // 8, 4]), ALU.mult))
                part(0, 2)
                steps.settle()
                ks = level_view(kt[:, :], 3, 0)
                dve.tensor_tensor(ks, ks, pairs[:, :, 1:2].to_broadcast([P, L // 16, 8]), ALU.mult)
                part(1, 3)
                steps.settle()
                steps.mark(dve.tensor_tensor(sixteens, pairs[:, :, 0], pairs[:, :, 1], ALU.mult))
                part(2, 3)
                qs = level_view(qt, 3, 1)
                dve.tensor_tensor(qs, qs, queries[:, :, 0:1].to_broadcast([P, SEQ // 16, 8]), ALU.mult) \
                    .then_inc(S["level_done"], 1)
                steps.settle()

            def states(r):
                dve.wait_ge(S["kv_mm"], r + 1)
                decay, _ = tree_at(LEVELS)
                steps.mark(dve.tensor_copy(st[:, 0:P], small[:, KVM]))
                for c in range(CHUNKS - 1):
                    steps.settle()
                    ins = dve.scalar_tensor_tensor(st[:, (c + 1) * P:(c + 2) * P], st[:, c * P:(c + 1) * P],
                                                   decay[:, c:c + 1], misc[c // 4][:, (c % 4) * P:(c % 4 + 1) * P],
                                                   ALU.mult, ALU.add)
                    if c < CHUNKS - 2:
                        steps.mark(ins)
                ins.then_inc(S["state_done"], 1)

            def normalise_o(r):
                dve.wait_ge(S["o_squared"], r + 1)
                steps.mark(dve.tensor_reduce(o_ss[:, :], ek[:, :].rearrange("p (c d) -> p c d", d=P), AX.X, ALU.add))
                steps.settle()
                dve.tensor_scalar(o_ms[:, :], o_ss[:, :], 1.0 / P, EPS, ALU.mult, ALU.add).then_inc(S["o_mean"], 1)
                dve.wait_ge(S["o_rstd"], r + 1)
                for q in range(2):
                    rs = o_rs[:, 4 * q:4 * q + 4].rearrange("p (c o) -> p c o", o=1).to_broadcast([P, 4, P])
                    ins = dve.tensor_tensor(on[:, q * HALF:(q + 1) * HALF].rearrange("p (c d) -> p c d", d=P),
                                            misc[q][:, :].rearrange("p (c d) -> p c d", d=P), rs, ALU.mult)
                ins.then_inc(S["o_normed"], 1)

            def gate(r, u, k):
                dve.wait_ge(S["acc_read"], u + (9 + k))
                g = gt[:, k * HALF:(k + 1) * HALF]
                dve.scalar_tensor_tensor(g, g, hgw[:, ds(r, 1)], gs[:, :], ALU.mult, ALU.mult) \
                    .then_inc(S["gate_done"], 1)

            def gated_o(r):
                dve.wait_ge(S["gate_done"], r * 2 + 2)
                dve.wait_ge(S["o_tr"], r + 1)
                for q in range(2):
                    s = slice(q * HALF, (q + 1) * HALF)
                    o = misc[q][:, :].rearrange("p (o t) -> p o t", o=1)
                    g = gt[:, s].rearrange("p (o t) -> p o t", o=1)
                    pr = prod[:, :].rearrange("p (o t) -> p o t", o=1)
                    after(dve, S["a_done"], r * 2 + q)
                    dve.tensor_tensor(a_hi[:, ds(r, 1), s], o, g, ALU.mult)
                    steps.mark(dve.tensor_tensor(pr, o, g, ALU.mult))
                    steps.settle()
                    dve.tensor_tensor(a_lo[:, ds(r, 1), s], pr, a_hi[:, ds(r, 1), s].bitcast(F32), ALU.subtract) \
                        .then_inc(S["a_done"], 1)

            steps.settle()
            split_lo(2, 0)
            prepare_gates(0, 7)
            split_lo(3, 1)

            def head_body(j, o_before):
                r, u, b = j - 1, j * 10, first_block(j)
                prepare(r)
                split_lo(b + 1, 0)
                level(r, 0)
                if o_before:
                    gated_o(r - 1)
                level(r, 1)
                split_lo(b + 2, 1)
                levels_2_and_3(r)
                level(r, 4)
                level(r, 5)
                split_lo(b + 3, 0)
                level(r, 6)
                states(r)
                prepare_gates(j, u + 3)
                split_lo(b + 4, 1)
                gate(r, u, 0)
                normalise_o(r)
                gate(r, u, 1)

            PER_HEAD = 4 + (3 + 8 + 15 + 2 + 3 + 2) + (CHUNKS - 1) + 1 + 2
            dve.wait_ge(S["masks_spread"], 1)
            head_body(1, False)
            with dve.Fori(2, HEADS) as j:
                steps.enter(j, 2, PER_HEAD)
                head_body(j, True)
            steps.leave(PER_HEAD, HEADS - 2)
            r, u, b = HEADS - 1, HEADS * 10, first_block(HEADS)
            prepare(r)
            split_lo(b + 1, 0)
            level(r, 0)
            gated_o(r - 1)
            level(r, 1)
            split_lo(b + 2, 1)
            levels_2_and_3(r)
            split_lo(b + 3, 0)
            level(r, 4)
            level(r, 5)
            split_lo(b + 4, 1)
            level(r, 6)
            states(r)
            split_lo(b + 5, 0)
            gate(r, u, 0)
            normalise_o(r)
            gate(r, u, 1)
            split_lo(BLK_TAIL + 1, 1)
            gated_o(r)
            for n in range(2, 5):
                split_lo(BLK_TAIL + n, n % 2)

            def mix_body(n, stored):
                b, u = n * 2 + BLK_MIX, n * 4 + U_MIX
                split_lo(b + 1, 1)
                split_lo(b + 2, 0)
                for h in range(2):
                    dve.wait_ge(S["acc_read"], u + (3 + h))
                    after(dve, part_stored[h], stored)
                    dve.tensor_tensor(part[:, h, :], sm[:, h, :], yb[:, h, :], ALU.mult).then_inc(S["part_made"], 1)

            mix_body(0, 0)
            with dve.Fori(1, NK) as n:
                mix_body(n, n * 16)

            def pooled(g, k, u):
                w, src = WINDOWS[g], uu[:, k, :]
                dve.wait_ge(S["acc_read"], u + 3 * (k + 1))
                after(dve, S["pooled_done"], 2 * g + k)
                after(dve, S["c_done"], 4 * g)
                bufs, s = [pool_a, pool_b], src
                for n in range(w.bit_length() - 1):
                    lo, step = (2 << n) - 1, 1 << n
                    dst = bufs[n % 2][:, :]
                    steps.mark(dve.tensor_tensor(dst[:, lo:L], s[:, lo:L], s[:, lo - step:L - step], ALU.add))
                    steps.settle()
                    s = dst
                tmp = bufs[(w.bit_length() - 1) % 2][:, META:L]
                dve.scalar_tensor_tensor(p_hi[:, k, :], s[:, META:L], 1.0 / w, src[:, META:L], ALU.mult, ALU.subtract)
                steps.mark(dve.scalar_tensor_tensor(tmp, s[:, META:L], 1.0 / w, src[:, META:L], ALU.mult,
                                                    ALU.subtract))
                steps.settle()
                dve.tensor_tensor(p_lo[:, k, :], tmp, p_hi[:, k, :].bitcast(F32), ALU.subtract) \
                    .then_inc(S["pooled_done"], 1)

            def pool_gate(g, k, u):
                dve.wait_ge(S["acc_read"], u + 7 + k)
                v = pg[:, k // 2, (k % 2) * HALF:(k % 2 + 1) * HALF]
                n = 2 * g + k // 2
                dve.scalar_tensor_tensor(v, v, psc[:, n:n + 1], pgs[:, :], ALU.mult, ALU.mult) \
                    .then_inc(S["pgate_done"], 1)

            for g in range(4):
                b, u = BLK_POOL + 4 * g, U_POOL + 14 * g
                split_lo(b + 1, 1)
                split_lo(b + 2, 0)
                pooled(g, 0, u)
                split_lo(b + 3, 1)
                pooled(g, 1, u)
                dve.wait_ge(S["pw_hi_done"], g + 1)
                dve.tensor_tensor(pw_lo[:, :], pw[:, :], pw_hi[:, :].bitcast(F32), ALU.subtract) \
                    .then_inc(S["pw_lo_done"], 1)
                pool_gate(g, 0, u)
                pool_gate(g, 1, u)
                split_lo(b + 4, 0)
                pool_gate(g, 2, u)
                pool_gate(g, 3, u)
                dve.wait_ge(S["pgate_done"], 4 * g + 4)
                for k in range(4):
                    n, s = 2 * g + k // 2, slice((k % 2) * HALF, (k % 2 + 1) * HALF)
                    dve.wait_ge(S["acc_read"], u + 11 + k)
                    after(dve, S["c_done"], 4 * g + k)
                    dve.wait_ge(S["pooled_done"], 2 * g + 2)
                    tmp = pool_a[:, 0:HALF]
                    dve.tensor_tensor(a_hi[:, n, s], mx[:, k % 2, :], pg[:, k // 2, s], ALU.mult)
                    steps.mark(dve.tensor_tensor(tmp, mx[:, k % 2, :], pg[:, k // 2, s], ALU.mult))
                    steps.settle()
                    dve.tensor_tensor(a_lo[:, n, s], tmp, a_hi[:, n, s].bitcast(F32), ALU.subtract) \
                        .then_inc(S["c_done"], 1)

            def merge(n, h):
                dve.wait_ge(S["acc_read"], n * 2 + (U_DOWN + h + 1))
                dve.wait_ge(spill_loaded[h], n * 32 + 32)
                s = slice(META + h * HALF, META + (h + 1) * HALF)
                one, hh = ds(n, 1), slice(h, h + 1)
                steps.mark(dve.tensor_tensor(mg[:, hh, :], yp[:, hh, :], sp_in[:, hh, :], ALU.mult))
                steps.settle()
                dve.tensor_tensor(h_hi[:, one, s], mg[:, hh, :], pt_in[:, hh, :], ALU.add)
                steps.mark(dve.tensor_tensor(mg[:, hh, :], mg[:, hh, :], pt_in[:, hh, :], ALU.add))
                steps.settle()
                dve.tensor_tensor(h_lo[:, one, s], mg[:, hh, :], h_hi[:, one, s].bitcast(F32), ALU.subtract) \
                    .then_inc(S["merged_done"], 1)

            PER_PAIR = 8
            with dve.Fori(0, NK // 2 - 1) as i:
                steps.enter(i, 0, PER_PAIR)
                for s in range(2):
                    split_lo(i * 2 + (BLK_DOWN + s + 1), 1 - s)
                    for h in range(2):
                        merge(i * 2 + s, h)
            steps.leave(PER_PAIR, NK // 2 - 1)
            split_lo(BLK_OUT - 1, 1)
            for n in range(NK - 2, NK):
                for q in range(2 * (n - NK + 2), 2 * (n - NK + 3)):
                    ks = slice(2 * q, 2 * q + 2)
                    split_lo(BLK_OUT + q, q % 2, wo0_lo[:, ks, :], wo0_hi[:, ks, :])
                for h in range(2):
                    merge(n, h)
            for q in range(4):
                ks = slice(2 * q, 2 * q + 2)
                split_lo(BLK_OUT + 4 + q, q % 2, wo1_lo[:, ks, :], wo1_hi[:, ks, :])

            def z_of(v):
                n, t = divmod(v, CHUNKS)
                return zz[:, t, :] if n == 0 else z1[:, t % 2, :]

            def add_residual(v):
                dve.wait_ge(S["acc_done"], U_OUT + v + 1)
                dve.wait_ge(xr_loaded[v % 2], 16 * (v // 2 + 1))
                after(dve, S["row_right_done"], v - CHUNKS - 1)
                dve.tensor_tensor(z_of(v), acc[v % 4][:, :], xr[:, v % 2, :], ALU.add).then_inc(S["z_done"], 1)

            def finish_rows(t):
                dve.wait_ge(S["z_squared"], t + 1)
                dve.tensor_tensor(zz[:, t, :], zz[:, t, :], fnw[:, 0:HALF], ALU.mult).then_inc(S["z_weighted"], 1)
                dve.wait_ge(S["z_squared"], CHUNKS + t + 1)
                one = slice(t, t + 1)
                steps.mark(dve.tensor_tensor(z_ms[:, one], z_ss[:, 0, one], z_ss[:, 1, one], ALU.add))
                steps.settle()
                dve.tensor_scalar(z_ms[:, one], z_ms[:, one], 1.0 / D, EPS, ALU.mult, ALU.add) \
                    .then_inc(S["z_mean"], 1)
                dve.wait_ge(S["z_rstd"], t + 1)
                after(dve, row_stored[t % 2], 16 * (t // 2))
                dve.scalar_tensor_tensor(row[:, t % 2, HALF:D], z1[:, t % 2, :], z_rs[:, one], fnw[:, HALF:D],
                                         ALU.mult, ALU.mult).then_inc(S["row_right_done"], 1)

            for v in range(CHUNKS):
                add_residual(v)
            dve.wait_ge(S["fnw_loaded"], 16)
            for v in range(CHUNKS, 2 * CHUNKS):
                add_residual(v)
                finish_rows(v - CHUNKS)


def kernel(**inputs):
    import numpy as np
    import concourse.bacc as bacc
    from concourse.bass_utils import run_bass_kernel_spmd

    def blocks(w):
        r, c = w.shape
        return w.reshape(r // P, P, c // P, P).transpose(2, 1, 0, 3).reshape(c // P, P, r)

    mats = {"in": blocks(inputs["w_in"][0]), "down_hg": blocks(inputs["w_down_hg"][0]),
            "down_pool": blocks(inputs["w_down_pool"][0])}
    mats["out"] = inputs["w_out"][0].reshape(4, 2, P, 2, HALF).transpose(3, 0, 2, 1, 4).reshape(8, P, D)
    arrays = {
        "x": inputs["x"][0],
        "meta": inputs["meta_tokens"],
        "norm_w": inputs["norm_w"],
        "wstream": np.stack([mats[m][n] for m, n in stream_order()]),
        "pool_w": inputs["pool_w"][0].reshape(4, 2, P, 256).transpose(0, 2, 1, 3).reshape(4, P, 512),
        "b_in": inputs["b_in"][0].reshape(8, 8, P).transpose(2, 1, 0),
        "lb_logits": inputs["lb_logits"].reshape(2, HEADS, P).transpose(2, 0, 1),
        "hg_norm_w": inputs["hg_norm_w"][0].reshape(HEADS, P).T,
        "pool_scale": inputs["pool_scale"][0].reshape(NK, P).T,
        "final_norm_w": inputs["final_norm_w"].reshape(1, D),
    }
    nc = bacc.Bacc("TRN2", target_bir_lowering=False, num_devices=1)
    fed, args = {}, {}
    for name, a in arrays.items():
        a = np.ascontiguousarray(a)
        fed[f"in_{name}"] = a
        args[name] = nc.dram_tensor(f"in_{name}", a.shape, mybir.dt.from_np(a.dtype), kind="ExternalInput").ap()
    args["out"] = nc.dram_tensor("out_z", (SEQ, D), F32, kind="ExternalOutput").ap()
    hybrid_block(nc, **args)
    r = run_bass_kernel_spmd(nc, [fed], core_ids=[0])
    return r.results[0]["out_z"].reshape(1, SEQ, D)
```
